# Optimizing a Trainium2 kernel written in Bass

```python
import jax
import jax.numpy as jnp
from jax import lax
import numpy as np

D_MODEL = 2048
BATCH = 1
SEQ = 256
DEPTH = 1

M_HEADS = 4
A_HEADS = 8
M_V_DIM = D_MODEL // 2 // M_HEADS
M_QK_DIM = M_V_DIM // 2
A_HEAD_DIM = D_MODEL // 2 // A_HEADS
M_CHUNK = 64
CONV_WIDTH = 4
GATE_CAP = 15.0
ATTN_PATTERNS = ((128, 1), (512, 4), (2048, 16))
ROPE_THETA = 10000.0
NORM_EPS = 1e-6
D_FF = ((8 * D_MODEL + 3 * 256 - 1) // (3 * 256)) * 256
M_QK_WIDTH = M_HEADS * M_QK_DIM
M_V_WIDTH = M_HEADS * M_V_DIM
A_WIDTH = A_HEADS * A_HEAD_DIM
MIX_WIDTH = M_V_WIDTH + A_WIDTH
SPLIT_SIZES = (M_QK_WIDTH, M_QK_WIDTH, M_V_WIDTH, M_V_WIDTH, M_HEADS, M_HEADS, A_WIDTH, A_WIDTH, A_WIDTH)
IN_WIDTH = 2 * M_QK_WIDTH + 2 * M_V_WIDTH + 2 * M_HEADS + 3 * A_WIDTH

kernel_name = "hymba_mlstm_dilated_swa_swiglu"

def rms_norm(x, w):
    xf = x.astype(jnp.float32)
    y = xf * lax.rsqrt(jnp.mean(xf * xf, axis=-1, keepdims=True) + NORM_EPS)
    return y * w.astype(jnp.float32)

def to_heads(t, n_heads):
    b, s, _ = t.shape
    return t.reshape(b, s, n_heads, -1).transpose(0, 2, 1, 3)

def from_heads(t):
    b, h, s, d = t.shape
    return t.transpose(0, 2, 1, 3).reshape(b, s, h * d)

def soft_cap(z):
    return GATE_CAP * jnp.tanh(z / GATE_CAP)

def causal_short_conv(x, w, b):
    k_width = w.shape[0]
    s = x.shape[1]
    xp = jnp.pad(x, ((0, 0), (k_width - 1, 0), (0, 0)))
    y = b
    for j in range(k_width):
        y = y + w[j] * xp[:, j:j + s]
    return y

def rope_tables(s, dim):
    inv_freq = ROPE_THETA ** (-jnp.arange(0, dim, 2, dtype=jnp.float32) / dim)
    ang = jnp.arange(s, dtype=jnp.float32)[:, None] * inv_freq[None, :]
    return jnp.cos(ang), jnp.sin(ang)

def apply_rope(x, cos, sin):
    half = x.shape[-1] // 2
    x1, x2 = x[..., :half], x[..., half:]
    return jnp.concatenate([x1 * cos - x2 * sin, x2 * cos + x1 * sin], axis=-1)

def mlstm_chunkwise(q, k, v, i_pre, f_pre):
    b, h, s, dk = q.shape
    dv = v.shape[-1]
    L = M_CHUNK
    nc = s // L
    q = q.reshape(b, h, nc, L, dk) * (dk ** -0.5)
    k = k.reshape(b, h, nc, L, dk)
    v = v.reshape(b, h, nc, L, dv)
    log_i = i_pre.reshape(b, h, nc, L)
    log_f = jax.nn.log_sigmoid(f_pre).reshape(b, h, nc, L)
    cum_f = jnp.cumsum(log_f, axis=-1)
    g = cum_f[..., -1]
    a = g[..., None] - cum_f + log_i
    m_loc = jnp.max(a, axis=-1)
    w_state = jnp.exp(a - m_loc[..., None])
    kv_c = jnp.einsum('bhcl,bhcld,bhcle->bhcde', w_state, k, v)
    n_c = jnp.einsum('bhcl,bhcld->bhcd', w_state, k)

    def step(carry, inp):
        c_st, n_st, m_st = carry
        kv, nn, ml, gg = inp
        m_new = jnp.maximum(gg + m_st, ml)
        s_old = jnp.exp(gg + m_st - m_new)
        s_new = jnp.exp(ml - m_new)
        c_new = s_old[..., None, None] * c_st + s_new[..., None, None] * kv
        n_new = s_old[..., None] * n_st + s_new[..., None] * nn
        return (c_new, n_new, m_new), (c_st, n_st, m_st)

    init = (jnp.zeros((b, h, dk, dv), jnp.float32), jnp.zeros((b, h, dk), jnp.float32),
            jnp.zeros((b, h), jnp.float32))
    xs = (jnp.moveaxis(kv_c, 2, 0), jnp.moveaxis(n_c, 2, 0), jnp.moveaxis(m_loc, 2, 0), jnp.moveaxis(g, 2, 0))
    _, (c_prev, n_prev, m_prev) = lax.scan(step, init, xs)
    c_prev = jnp.moveaxis(c_prev, 0, 2)
    n_prev = jnp.moveaxis(n_prev, 0, 2)
    m_prev = jnp.moveaxis(m_prev, 0, 2)

    causal = jnp.tril(jnp.ones((L, L), dtype=bool))
    d_log = cum_f[..., :, None] - cum_f[..., None, :] + log_i[..., None, :]
    d_log = jnp.where(causal, d_log, -jnp.inf)
    inter_log = cum_f + m_prev[..., None]
    m_t = jnp.maximum(inter_log, jnp.max(d_log, axis=-1))
    p_intra = jnp.exp(d_log - m_t[..., None])
    w_inter = jnp.exp(inter_log - m_t)
    s_qk = jnp.einsum('bhctd,bhcsd->bhcts', q, k) * p_intra
    num = (w_inter[..., None] * jnp.einsum('bhctd,bhcde->bhcte', q, c_prev)
           + jnp.einsum('bhcts,bhcse->bhcte', s_qk, v))
    den = w_inter * jnp.einsum('bhctd,bhcd->bhct', q, n_prev) + jnp.sum(s_qk, axis=-1)
    out = num / jnp.maximum(jnp.abs(den), jnp.exp(-m_t))[..., None]
    return out.reshape(b, h, s, dv)

def dilated_window_attention(q, k, v, window, dilation):
    b, h, s, dh = q.shape
    w_sub = window // dilation
    L = s // dilation
    nb = -(-L // w_sub)
    lp = nb * w_sub

    def to_sub(t):
        t = t.reshape(b, h, L, dilation, dh).transpose(0, 1, 3, 2, 4)
        return jnp.pad(t, ((0, 0), (0, 0), (0, 0), (0, lp - L), (0, 0)))

    def band(t):
        t = jnp.pad(t, ((0, 0), (0, 0), (0, 0), (w_sub, 0), (0, 0))).reshape(b, h, dilation, nb + 1, w_sub, dh)
        return jnp.concatenate([t[:, :, :, :-1], t[:, :, :, 1:]], axis=4)

    qb = to_sub(q).reshape(b, h, dilation, nb, w_sub, dh)
    kb = band(to_sub(k))
    vb = band(to_sub(v))
    scores = jnp.einsum('bhrnqd,bhrnkd->bhrnqk', qb, kb) * (dh ** -0.5)
    qi = jnp.arange(w_sub)[:, None]
    kj = jnp.arange(2 * w_sub)[None, :]
    blk = jnp.arange(nb)[:, None, None]
    dist = qi + w_sub - kj
    valid = (dist >= 0) & (dist <= w_sub) & (blk * w_sub + kj - w_sub >= 0)
    scores = jnp.where(valid, scores, -jnp.inf)
    m = jnp.max(scores, axis=-1, keepdims=True)
    p = jnp.exp(scores - m)
    den = jnp.sum(p, axis=-1)
    o = jnp.einsum('bhrnqk,bhrnkd->bhrnqd', p, vb) / den[..., None]
    lse = m[..., 0] + jnp.log(den)
    o = o.reshape(b, h, dilation, lp, dh)[:, :, :, :L].transpose(0, 1, 3, 2, 4).reshape(b, h, s, dh)
    lse = lse.reshape(b, h, dilation, lp)[:, :, :, :L].transpose(0, 1, 3, 2).reshape(b, h, s)
    return o, lse

def setup_inputs(seed: int = 0) -> dict:
    key = jax.random.key(seed)
    ks = jax.random.split(key, 20)
    f32 = jnp.float32

    def nrm(k, shape, scale):
        return jax.random.normal(k, shape, f32) * scale

    return {
        "x": nrm(ks[0], (BATCH, SEQ, D_MODEL), 1.0),
        "norm1_w": 1.0 + nrm(ks[1], (DEPTH, D_MODEL), 0.02),
        "w_in": nrm(ks[2], (DEPTH, D_MODEL, IN_WIDTH), D_MODEL ** -0.5),
        "conv_w": nrm(ks[3], (DEPTH, CONV_WIDTH, 2 * M_QK_WIDTH), CONV_WIDTH ** -0.5),
        "conv_b": nrm(ks[4], (DEPTH, 2 * M_QK_WIDTH), 0.01),
        "igate_b": nrm(ks[5], (DEPTH, M_HEADS), 0.1),
        "fgate_b": jnp.linspace(3.0, 6.0, M_HEADS, dtype=f32) + nrm(ks[6], (DEPTH, M_HEADS), 0.1),
        "q_norm_w": 1.0 + nrm(ks[7], (DEPTH, A_HEAD_DIM), 0.02),
        "k_norm_w": 1.0 + nrm(ks[8], (DEPTH, A_HEAD_DIM), 0.02),
        "mlstm_norm_w": 1.0 + nrm(ks[9], (DEPTH, M_HEADS, M_V_DIM), 0.02),
        "attn_norm_w": 1.0 + nrm(ks[10], (DEPTH, A_HEADS, A_HEAD_DIM), 0.02),
        "w_out": nrm(ks[11], (DEPTH, MIX_WIDTH, D_MODEL), MIX_WIDTH ** -0.5),
        "norm2_w": 1.0 + nrm(ks[12], (DEPTH, D_MODEL), 0.02),
        "w_gate": nrm(ks[13], (DEPTH, D_MODEL, D_FF), D_MODEL ** -0.5),
        "w_up": nrm(ks[14], (DEPTH, D_MODEL, D_FF), D_MODEL ** -0.5),
        "w_down": nrm(ks[15], (DEPTH, D_FF, D_MODEL), D_FF ** -0.5),
    }

def reference(x, norm1_w, w_in, conv_w, conv_b, igate_b, fgate_b, q_norm_w, k_norm_w,
              mlstm_norm_w, attn_norm_w, w_out, norm2_w, w_gate, w_up, w_down):
    dtype = x.dtype
    s = x.shape[1]
    cos, sin = rope_tables(s, A_HEAD_DIM)
    split_points = np.cumsum(SPLIT_SIZES)[:-1].tolist()
    h = x
    for l in range(DEPTH):
        u = rms_norm(h, norm1_w[l]).astype(dtype)
        proj = jnp.matmul(u, w_in[l]).astype(jnp.float32)
        mq, mk, mv, mo, mi, mf, aq, ak, av = jnp.split(proj, split_points, axis=-1)

        qk = jax.nn.silu(causal_short_conv(jnp.concatenate([mq, mk], axis=-1),
                                           conv_w[l].astype(jnp.float32), conv_b[l].astype(jnp.float32)))
        mq, mk = qk[..., :M_QK_WIDTH], qk[..., M_QK_WIDTH:]
        i_pre = soft_cap(mi + igate_b[l].astype(jnp.float32)).transpose(0, 2, 1)
        f_pre = soft_cap(mf + fgate_b[l].astype(jnp.float32)).transpose(0, 2, 1)
        hm = mlstm_chunkwise(to_heads(mq, M_HEADS), to_heads(mk, M_HEADS), to_heads(mv, M_HEADS), i_pre, f_pre)
        hm = rms_norm(hm, mlstm_norm_w[l][:, None, :])
        hm = from_heads(hm) * jax.nn.sigmoid(mo)

        qa = apply_rope(rms_norm(to_heads(aq, A_HEADS), q_norm_w[l]), cos, sin)
        ka = apply_rope(rms_norm(to_heads(ak, A_HEADS), k_norm_w[l]), cos, sin)
        va = to_heads(av, A_HEADS)
        outs = []
        lses = []
        for window, dilation in ATTN_PATTERNS:
            o_p, lse_p = dilated_window_attention(qa, ka, va, window, dilation)
            outs.append(o_p)
            lses.append(lse_p)
        alpha = jax.nn.softmax(jnp.stack(lses, axis=0), axis=0)
        ha = jnp.einsum('pbhs,pbhsd->bhsd', alpha, jnp.stack(outs, axis=0))
        ha = from_heads(rms_norm(ha, attn_norm_w[l][:, None, :]))

        mix = jnp.concatenate([hm, ha], axis=-1).astype(dtype)
        h = h + jnp.matmul(mix, w_out[l])

        u2 = rms_norm(h, norm2_w[l]).astype(dtype)
        ff = jax.nn.silu(jnp.matmul(u2, w_gate[l])) * jnp.matmul(u2, w_up[l])
        h = h + jnp.matmul(ff, w_down[l])
    return h.astype(dtype)


_drawn_inputs = setup_inputs


def setup_inputs(seed=0):
    import zlib

    import numpy as np

    out = dict(_drawn_inputs(seed))
    spreads = {}
    factors = {'conv_b': 8.0,
     'igate_b': 64.0,
     'q_norm_w': 4.916,
     'k_norm_w': 4.99,
     'mlstm_norm_w': 80.169,
     'attn_norm_w': 44.645,
     'norm2_w': 12.811}
    for name, (base, spread) in spreads.items():
        noise = np.random.default_rng([zlib.crc32(name.encode()), seed]).standard_normal(out[name].shape)
        drawn = base * np.exp(spread * noise) if base else spread * noise
        out[name] = jnp.asarray(drawn.astype(out[name].dtype))
    for name, factor in factors.items():
        out[name] = (out[name] * factor).astype(out[name].dtype)
    return out
```

```python
from contextlib import ExitStack

import numpy as np
import concourse.bass as bass
from concourse import mybir

F32 = mybir.dt.float32
F32R = mybir.dt.float32r
ALU = mybir.AluOpType
ACT = mybir.ActivationFunctionType
AX = mybir.AxisListType

P = 128
D = 2048
S = 256
NJ = S // P
KD = D // P
MH, MQ, MV = 4, 128, 256
AH, AD = 8, 128
GATE_CAP = 15.0
EPS = 1e-6
FF = 5632
COLS = 512
PIECE = 4
CHUNK = 2
PIECES = 4
CHUNKS_AHEAD = 4
OFF_MQ, OFF_MK, OFF_MV, OFF_MO, OFF_GATES = 0, 512, 1024, 2048, 3072
OFF_AQ, OFF_AK, OFF_AV = 3080, 4104, 5128
IN_BLOCKS = [OFF_AQ, OFF_AQ + COLS, OFF_AK, OFF_AK + COLS, OFF_AV, OFF_AV + COLS,
             OFF_MQ, OFF_MK, OFF_MV, OFF_MV + COLS, OFF_MO, OFF_MO + COLS]
IN_CH = KD // CHUNK
OUT0 = len(IN_BLOCKS) * IN_CH
OUT_CH = KD // 2 // CHUNK
NB = D // COLS
OUT1 = OUT0 + NB * OUT_CH
FFN0 = OUT1 + NB * OUT_CH
GROUPS = FF // COLS
G0, U0, G1, U1 = (FFN0 + IN_CH * n for n in range(4))
LOOP0 = FFN0 + 4 * IN_CH
PER_GROUP = 3 * IN_CH
TAIL0 = LOOP0 + PER_GROUP * (GROUPS - 2)
CHUNKS = TAIL0 + 2 * IN_CH
C_N1, C_N2, C_MN, C_AN, C_CW, C_CB, C_ALL = 0, 16, 32, 40, 48, 80, 88
K_ID, K_COS, K_SIN, K_NEG, K_W, K_L, K_U, K_NU, K_ALL = 0, 128, 256, 384, 640, 1024, 1152, 1280, 1408
NEG = -1e30
NHEAD_SLOT = 42
DEC_SLOT = 61
MS_SLOT = 71
MP_SLOT = 82


def constants():
    c = np.zeros((P, K_ALL), np.float32)
    r = np.arange(P)
    c[:, K_ID:K_COS] = np.eye(P)
    inv = (np.float32(10000.0) ** (-np.arange(0, AD, 2, dtype=np.float32) / np.float32(AD))).astype(np.float32)
    ang = np.arange(S, dtype=np.float32)[:, None] * inv[None, :]
    for j in range(NJ):
        a = ang[j * P:(j + 1) * P].astype(np.float64)
        c[:, K_COS + 64 * j:K_COS + 64 * j + 64] = np.cos(a)
        c[:, K_SIN + 64 * j:K_SIN + 64 * j + 64] = np.sin(a)
    t, s = np.arange(S)[:, None], np.arange(S)[None, :]
    d = t - s
    seen = ((d >= 0) & (d <= 128)) * 1 + ((d >= 0) & (d % 4 == 0)) * 1 + ((d >= 0) & (d % 16 == 0)) * 1
    c[:, K_NEG:K_W] = np.where(seen[P:] > 0, 0.0, NEG)
    c[:, K_W:K_W + P] = seen[:P, :P].T
    c[:, K_W + P:K_W + 2 * P] = seen[P:, :P].T
    c[:, K_W + 2 * P:K_W + 3 * P] = seen[P:, P:].T
    c[:, K_L:K_U] = r[:, None] > r[None, :]
    c[:, K_U:K_NU] = r[:, None] <= r[None, :]
    c[:, K_NU:K_ALL] = np.where(r[:, None] > r[None, :], NEG, 0.0)
    return c


def build(nc, x, norm1_w, w_in, conv_w, conv_b, igate_b, fgate_b, q_norm_w, k_norm_w,
          mlstm_norm_w, attn_norm_w, w_out, norm2_w, w_gate, w_up, w_down, consts, out):
    with ExitStack() as ctx:
        def sb(name, shape, dt=F32):
            return ctx.enter_context(nc.sbuf_tensor(name, shape, dt))

        def sem(name):
            return ctx.enter_context(nc.semaphore(name))

        h = sb("h", [P, NJ, D])
        raw = sb("raw", [P, PIECES, PIECE, COLS])
        w_hi = sb("w_hi", [P, CHUNKS_AHEAD, CHUNK, COLS], F32R)
        w_lo = sb("w_lo", [P, CHUNKS_AHEAD, CHUNK, COLS], F32R)
        t_hi = sb("t_hi", [P, KD, S], F32R)
        t_lo = sb("t_lo", [P, KD, S], F32R)
        a_hi = sb("a_hi", [P, KD // 2, S], F32R)
        a_lo = sb("a_lo", [P, KD // 2, S], F32R)
        ff_hi = sb("ff_hi", [P, PIECE, S], F32R)
        ff_lo = sb("ff_lo", [P, PIECE, S], F32R)
        con = sb("con", [P, K_ALL])
        par = sb("par", [P, C_ALL])
        qk_w = sb("qk_w", [P, 2, AD])
        rope_w = sb("rope_w", [P, 4, NJ, 64])
        wg_raw = sb("wg_raw", [P, KD, 8])
        wg_hi = sb("wg_hi", [P, KD, 8], F32R)
        wg_lo = sb("wg_lo", [P, KD, 8], F32R)
        gate_b = sb("gate_b", [P, 8])
        area1 = sb("area1", [P, 3584])
        area2 = sb("area2", [P, 2 * NJ * MH * (MV + 1)])
        v_tok = sb("v_tok", [P, NJ, AH, AD + 1])
        ha = sb("ha", [P, NJ, AH, AD + 1])
        seg = sb("seg", [P, NJ, MH, P])
        area6 = sb("area6", [P, 4 * (S + 3)])
        sc = sb("sc", [P, 2, 3 * P])
        p_t = sb("p_t", [P, 3 * P])
        small = sb("small", [P, 256])
        r_row = sb("r_row", [P, S])

        tok = area1[:, 0:1024].rearrange("p (j h d) -> p j h d", j=NJ, h=4)
        rot = area1[:, 1024:2048].rearrange("p (j h d) -> p j h d", j=NJ, h=4)
        sq = area1[:, 2048:3072].rearrange("p (j h d) -> p j h d", j=NJ, h=4)
        param_rows = area1[0:C_ALL, 3072:3200]
        squares = area1[:, 0:2048]
        mqk = area1[:, 0:2048].rearrange("p (h t) -> p h t", h=8)
        dec = area1[:, 2048:3584].rearrange("p (h t) -> p h t", h=MH)
        g_act = area1[:, 0:1024].rearrange("p (j c) -> p j c", j=NJ)
        ff = area1[:, 1024:2048].rearrange("p (j c) -> p j c", j=NJ)
        q_t = area2[:, 0:2048].rearrange("p (h t) -> p h t", h=AH)
        k_t = area2[:, 2048:4096].rearrange("p (h t) -> p h t", h=AH)
        half = NJ * MH * (MV + 1)
        mv = area2[:, 0:half].rearrange("p (j h d) -> p j h d", j=NJ, h=MH)
        hm = area2[:, half:2 * half].rearrange("p (j h d) -> p j h d", j=NJ, h=MH)
        ha_sq = area2[:, half:half + 2048].rearrange("p (j h d) -> p j h d", j=NJ, h=AH)
        o_sig = v_tok[:, :, :, :].rearrange("p j h d -> p (j h d)")[:, 0:2048].rearrange("p (j c) -> p j c", j=NJ)
        conv_x = area6[:, :].rearrange("p (c t) -> p c t", c=4)
        rope_a = area6[:, 0:512].rearrange("p (j h d) -> p j h d", j=NJ, h=4)
        rope_b = area6[:, 512:1024].rearrange("p (j h d) -> p j h d", j=NJ, h=4)
        g_row = area1[0:MH, 3072:3584].rearrange("p (k t) -> p k t", k=2)
        m_row = rope_w[0:MH, :, :, :].rearrange("p k j d -> p (k j d)").rearrange("p (k t) -> p k t", k=2)
        ident = con[:, K_ID:K_ID + P]
        upper = con[:, K_U:K_U + P]

        used = [0]

        def col(n):
            used[0] += n
            assert used[0] <= 256
            return small[:, used[0] - n:used[0]]

        ss1, r1, ss2, s2sum, r2 = col(2), col(2), col(8), col(2), col(2)
        qss, a_max, a_neg = col(8), col(2 * 2), col(2 * 2)
        a_ss, a_rd, a_r = col(16), col(16), col(16)
        z, lg, e_f, u_f, c_f, ru_f, ln_f, lf = col(16), col(16), col(8), col(8), col(8), col(8), col(8), col(8)
        m_exp, m_ss, m_den, m_rd, m_r = col(8), col(8), col(8), col(8), col(8)
        one = col(1)

        bank = [ctx.enter_context(nc.psum_tensor(f"bank{i}", [P, COLS], F32)) for i in range(8)]

        piece_landed = [sem(f"piece_landed{i}") for i in range(PIECES)]
        x_landed = [sem(f"x_landed{i}") for i in range(4)]
        con_landed, par_landed, side_landed = sem("con_landed"), sem("par_landed"), sem("side_landed")
        hi_ready, lo_ready, chunk_used = sem("hi_ready"), sem("lo_ready"), sem("chunk_used")
        padded = sem("padded")
        par_turned, par_ready = sem("par_turned"), sem("par_ready")
        x_turned, u_hi, u_lo = sem("x_turned"), sem("u_hi"), sem("u_lo")
        x_squared, x_mean, x_root, r1_ready = sem("x_squared"), sem("x_mean"), sem("x_root"), sem("r1_ready")
        r_spread, r_row_ready = sem("r_spread"), sem("r_row_ready")
        wg_hi_ready, wg_lo_ready = sem("wg_hi_ready"), sem("wg_lo_ready")
        evacuated = sem("evacuated")
        qk_squared, qk_mean, qk_root, roped = sem("qk_squared"), sem("qk_mean"), sem("qk_root"), sem("roped")
        qk_turned, qk_out = sem("qk_turned"), sem("qk_out")
        a_scored, a_masked, a_exped = sem("a_scored"), sem("a_masked"), sem("a_exped")
        a_turned, a_weighted, a_summed, a_out = sem("a_turned"), sem("a_weighted"), sem("a_summed"), sem("a_out")
        a_squared, a_mean, a_root, a_normed = sem("a_squared"), sem("a_mean"), sem("a_root"), sem("a_normed")
        ha_turned, ha_hi, ha_lo = sem("ha_turned"), sem("ha_hi"), sem("ha_lo")
        g_summed, g_z, g_tanh, g_capped = sem("g_summed"), sem("g_z"), sem("g_tanh"), sem("g_capped")
        g_exped, g_plus1, g_logged, g_logf = sem("g_exped"), sem("g_plus1"), sem("g_logged"), sem("g_logf")
        g_turned, g_rows, m_scanned, m_turned, m_exped = (sem("g_turned"), sem("g_rows"), sem("m_scanned"),
                                                          sem("m_turned"), sem("m_exped"))
        seg_ready, d_summed, d_exped = sem("seg_ready"), sem("d_summed"), sem("d_exped")
        conv_x_ready, conv_done, conv_silu = sem("conv_x_ready"), sem("conv_done"), sem("conv_silu")
        m_scored, m_decayed, m_summed, m_out = sem("m_scored"), sem("m_decayed"), sem("m_summed"), sem("m_out")
        m_squared, m_mean, m_root, m_normed = sem("m_squared"), sem("m_mean"), sem("m_root"), sem("m_normed")
        hm_turned, hm_hi, hm_lo = sem("hm_turned"), sem("hm_hi"), sem("hm_lo")
        out_added, h_squared, h_turned, u2_hi, u2_lo = (sem("out_added"), sem("h_squared"), sem("h_turned"),
                                                        sem("u2_hi"), sem("u2_lo"))
        h_mean, h_root, r2_ready = sem("h_mean"), sem("h_root"), sem("r2_ready")
        gated, ff_ready, ff_turned, ff_hi_ready, ff_lo_ready = (sem("gated"), sem("ff_ready"), sem("ff_turned"),
                                                                sem("ff_hi_ready"), sem("ff_lo_ready"))
        down_added, stored, settled = sem("down_added"), sem("stored"), sem("settled")

        block = ctx.enter_context(nc.Block())

        @block.sync
        def _(sp):
            def load(p, src, slot):
                if not isinstance(p, int) or p >= PIECES:
                    sp.wait_ge(lo_ready, p * 2 - 2 * PIECES + 2)
                sp.dma_start(raw[:, slot, :, :], src).then_inc(piece_landed[slot], 16)

            def rows(w, first, c0):
                return w[0, first:first + PIECE * P, c0:c0 + COLS].rearrange("(t p) c -> p t c", p=P)

            def load_x(n):
                sp.dma_start(h[:, :, n * COLS:(n + 1) * COLS],
                             x[0, :, n * COLS:(n + 1) * COLS].rearrange("(j p) c -> p j c", p=P)
                             ).then_inc(x_landed[n], 16)

            p = 0
            for c0 in IN_BLOCKS:
                for q in range(KD // PIECE):
                    if p < 4:
                        load_x(p)
                    load(p, rows(w_in, q * PIECE * P, c0), p % PIECES)
                    p += 1
            for first in (D // 2, 0):
                for n in range(NB):
                    for q in range(KD // 2 // PIECE):
                        load(p, rows(w_out, first + q * PIECE * P, n * COLS), p % PIECES)
                        p += 1

            gate_v = w_gate[0].rearrange("(q t p) (g c) -> g q p t c", p=P, t=PIECE, c=COLS)
            up_v = w_up[0].rearrange("(q t p) (g c) -> g q p t c", p=P, t=PIECE, c=COLS)
            down_v = w_down[0].rearrange("(g t p) (n c) -> g n p t c", p=P, t=PIECE, c=COLS)

            for g in range(2):
                for v in (gate_v, up_v):
                    for q in range(4):
                        load(p, v[g, q], p % PIECES)
                        p += 1
            assert p == LOOP0 // 2
            with sp.Fori(1, GROUPS - 1) as i:
                for k, (v, g) in enumerate(((down_v, i - 1), (gate_v, i + 1), (up_v, i + 1))):
                    for q in range(4):
                        load(i * (PER_GROUP // 2) + (p - PER_GROUP // 2 + 4 * k + q), v[g, q], q)
            p = TAIL0 // 2
            for g in (GROUPS - 2, GROUPS - 1):
                for q in range(4):
                    load(p, down_v[g, q], p % PIECES)
                    p += 1
            for n in range(NB):
                sp.wait_ge(down_added, NB * (GROUPS - 1) + n + 1)
                sp.dma_start(out[0, :, n * COLS:(n + 1) * COLS].rearrange("(j p) c -> p j c", p=P),
                             h[:, :, n * COLS:(n + 1) * COLS]).then_inc(stored, 16)
            sp.wait_ge(stored, 16 * NB)

        @block.gpsimd
        def _(pool):
            pool.memset(one, 1.0).then_inc(padded, 1)
            pool.memset(v_tok[:, :, :, AD:AD + 1], 1.0).then_inc(padded, 1)
            pool.dma_start(wg_raw[:, :, :], w_in[0, :, OFF_GATES:OFF_GATES + 8].rearrange("(t p) c -> p t c", p=P)
                           ).then_inc(side_landed, 16)
            pool.dma_start(gate_b[:, 0:MH], igate_b.partition_broadcast(P).rearrange("p o c -> p (o c)")
                           ).then_inc(side_landed, 16)
            pool.dma_start(gate_b[:, MH:8], fgate_b.partition_broadcast(P).rearrange("p o c -> p (o c)")
                           ).then_inc(side_landed, 16)
            pool.dma_start(qk_w[:, 0, :], q_norm_w.partition_broadcast(P).rearrange("p o c -> p (o c)")
                           ).then_inc(side_landed, 16)
            pool.dma_start(qk_w[:, 1, :], k_norm_w.partition_broadcast(P).rearrange("p o c -> p (o c)")
                           ).then_inc(side_landed, 16)

        @block.scalar
        def _(act):
            act.dma_start(param_rows[C_N1:C_N2, :], norm1_w.rearrange("o (t p) -> (o t) p", p=P)).then_inc(par_landed, 16)
            act.dma_start(con[:, :], consts).then_inc(con_landed, 16)
            act.dma_start(param_rows[C_N2:C_MN, :], norm2_w.rearrange("o (t p) -> (o t) p", p=P)).then_inc(par_landed, 16)
            act.dma_start(param_rows[C_MN:C_AN, :], mlstm_norm_w.rearrange("o h (t p) -> (o h t) p", p=P)).then_inc(par_landed, 16)
            act.dma_start(param_rows[C_AN:C_CW, :], attn_norm_w.rearrange("o h p -> (o h) p")).then_inc(par_landed, 16)
            act.dma_start(param_rows[C_CW:C_CB, :], conv_w.rearrange("o w (t p) -> (o w t) p", p=P)).then_inc(par_landed, 16)
            act.dma_start(param_rows[C_CB:C_ALL, :], conv_b.rearrange("o (t p) -> (o t) p", p=P)).then_inc(par_landed, 16)

            def split(c, landed, slot):
                if slot % 2 == 0:
                    act.wait_ge(piece_landed[slot // 2], landed)
                if not isinstance(c, int) or c >= CHUNKS_AHEAD:
                    act.wait_ge(chunk_used, c - (CHUNKS_AHEAD - 1))
                act.activation(w_hi[:, slot % 4, :, :], raw[:, slot // 2, 2 * (slot % 2):2 * (slot % 2) + 2, :],
                               ACT.Copy).then_inc(hi_ready, 1)

            def split_at(c):
                if c < CHUNKS:
                    split(c, 16 * (c // 8 + 1), c % 8)

            def u_part(c):
                act.wait_ge(x_turned, c + 1)
                for k in range(2):
                    act.activation(t_hi[:, 2 * c + k, :], bank[4 + c % 4][:, S * k:S * k + S], ACT.Copy,
                                   scale=par[:, C_N1 + 2 * c + k:C_N1 + 2 * c + k + 1]).then_inc(u_hi, 1)

            def ff_part(g):
                for b in range(2):
                    act.wait_ge(ff_turned, g * 2 + b + 1)
                    act.activation(ff_hi[:, 2 * b:2 * b + 2, :], bank[2 + b][:, :].rearrange("p (k t) -> p k t", k=2),
                                   ACT.Copy).then_inc(ff_hi_ready, 1)

            def gate_silu(g):
                act.wait_ge(ff_ready, g)
                for j in range(NJ):
                    act.activation(g_act[:, j, :], bank[j][:, :], ACT.Silu, scale=r2[:, j:j + 1]).then_inc(gated, 1)

            act.wait_ge(par_turned, 1)
            act.activation(par[:, :], bank[2][:, 0:C_ALL], ACT.Copy).then_inc(par_ready, 1)
            act.wait_ge(par_ready, 1)
            for c in range(CHUNKS_AHEAD):
                u_part(c)
                split_at(c)
            for s in range(LOOP0):
                if s < 4:
                    u_part(s + 4)
                if s in (4, 5):
                    j = s - 4
                    act.wait_ge(par_turned, 1)
                    for n in range(4):
                        act.wait_ge(x_landed[n], 16)
                    act.wait_ge(x_squared, j)
                    act.activation(squares, h[:, j, :], ACT.Square, accum_out=ss1[:, j:j + 1]).then_inc(x_squared, 1)
                if s == 6:
                    act.wait_ge(x_mean, 1)
                    act.activation(ss1, ss1, ACT.Sqrt).then_inc(x_root, 1)
                if s == 7:
                    act.wait_ge(side_landed, 16 * 5)
                    act.activation(wg_hi[:, :, :], wg_raw[:, :, :], ACT.Copy).then_inc(wg_hi_ready, 1)
                if s in (16, 24, 32, 40):
                    b = s // 8 - 2
                    dst = q_t if b < 2 else k_t
                    for n in range(2):
                        act.wait_ge(qk_turned, 2 * b + n + 1)
                        act.activation(dst[:, 4 * (b % 2) + 2 * n:4 * (b % 2) + 2 * n + 2, :],
                                       bank[4 + n][:, :].rearrange("p (h t) -> p h t", h=2), ACT.Copy).then_inc(qk_out, 1)
                if s in (8, 16, 24, 32):
                    b = s // 8 - 1
                    act.wait_ge(chunk_used, s)
                    act.wait_ge(r1_ready, 1)
                    if b:
                        act.wait_ge(roped, b)
                    for j in range(NJ):
                        act.activation(tok[:, j, :, :], bank[2 * (b % 2) + j][:, :].rearrange("p (h d) -> p h d", h=4),
                                       ACT.Copy, scale=r1[:, j:j + 1]).then_inc(evacuated, 1)
                if s in (9, 17, 25, 33):
                    b = s // 8 - 1
                    act.wait_ge(evacuated, 2 * b + 2)
                    act.activation(sq, tok, ACT.Square).then_inc(qk_squared, 1)
                if s in (11, 19, 27, 35):
                    b = s // 8 - 1
                    act.wait_ge(qk_mean, b + 1)
                    act.activation(qss, qss, ACT.Sqrt).then_inc(qk_root, 1)
                if s in (40, 48):
                    b = s // 8 - 1
                    act.wait_ge(chunk_used, s)
                    act.wait_ge(padded, 2)
                    for j in range(NJ):
                        act.activation(v_tok[:, j, 4 * (b - 4):4 * (b - 4) + 4, 0:AD],
                                       bank[2 * (b % 2) + j][:, :].rearrange("p (h d) -> p h d", h=4),
                                       ACT.Copy, scale=r1[:, j:j + 1]).then_inc(evacuated, 1)
                if s >= NHEAD_SLOT + 6 and (s - NHEAD_SLOT) % 3 == 0 and (s - NHEAD_SLOT - 6) // 3 < AH:
                    n = (s - NHEAD_SLOT - 6) // 3
                    act.wait_ge(a_summed, n + 1)
                    act.activation(ha[:, :, n, :], bank[6][:, 0:2 * (AD + 1)].rearrange("p (j d) -> p j d", j=NJ),
                                   ACT.Copy).then_inc(a_out, 1)
                if s >= NHEAD_SLOT + 2 and (s - NHEAD_SLOT) % 3 == 2 and (s - NHEAD_SLOT - 2) // 3 < AH:
                    n = (s - NHEAD_SLOT - 2) // 3
                    act.wait_ge(a_masked, n + 1)
                    act.activation(sc[:, n % 2, 0:P], sc[:, n % 2, 0:P], ACT.Exp,
                                   bias=a_neg[:, 2 * (n % 2):2 * (n % 2) + 1]).then_inc(a_exped, 1)
                    act.activation(sc[:, n % 2, P:3 * P], sc[:, n % 2, P:3 * P], ACT.Exp,
                                   bias=a_neg[:, 2 * (n % 2) + 1:2 * (n % 2) + 2]).then_inc(a_exped, 1)
                if s == 70:
                    act.wait_ge(a_out, AH)
                    for j in range(NJ):
                        act.activation(ha_sq[:, j, :, :], ha[:, j, :, 0:AD], ACT.Square).then_inc(a_squared, 1)
                if s == 73:
                    act.wait_ge(a_mean, 1)
                    act.activation(a_ss, a_ss, ACT.Sqrt).then_inc(a_root, 1)
                if s in (77, 80):
                    n = (s - 77) // 3
                    for k in range(4):
                        if k % 2 == 0:
                            act.wait_ge(ha_turned, 2 * n + k // 2 + 1)
                        ch = 4 * n + k
                        act.activation(a_hi[:, ch, :], bank[5 + k // 2][:, S * (k % 2):S * (k % 2) + S], ACT.Copy,
                                       scale=par[:, C_AN + ch:C_AN + ch + 1]).then_inc(ha_hi, 1)
                if s == 50:
                    act.wait_ge(g_z, 2)
                    act.activation(z, z, ACT.Tanh, scale=1.0 / GATE_CAP).then_inc(g_tanh, 1)
                if s == 52:
                    act.wait_ge(g_capped, 1)
                    act.activation(e_f.rearrange("p (j h) -> p j h", j=NJ),
                                   lg.rearrange("p (j h) -> p j h", j=NJ)[:, :, MH:8], ACT.Exp, scale=-1.0).then_inc(g_exped, 1)
                if s == 54:
                    act.wait_ge(g_plus1, 1)
                    act.activation(ln_f, u_f, ACT.Ln).then_inc(g_logged, 1)
                if s == 57:
                    act.wait_ge(g_turned, 1)
                    act.activation(g_row[:, 0:2, :], bank[7][0:MH, :].rearrange("p (k t) -> p k t", k=2), ACT.Copy).then_inc(g_rows, 1)
                if s == 60:
                    act.wait_ge(m_turned, 1)
                    act.activation(m_exp, bank[7][:, 0:8], ACT.Exp, scale=-1.0).then_inc(m_exped, 1)
                if s in (61, 69):
                    n = (s - 61) // 8
                    act.wait_ge(conv_done, 4 * n + 4)
                    act.activation(mqk[:, 4 * n:4 * n + 4, :], mqk[:, 4 * n:4 * n + 4, :], ACT.Silu).then_inc(conv_silu, 1)
                if DEC_SLOT < s < DEC_SLOT + 2 * MH and (s - DEC_SLOT) % 2 == 1:
                    n = (s - DEC_SLOT) // 2
                    act.wait_ge(d_summed, n + 1)
                    act.activation(dec[:, n, 0:S], bank[7][:, 0:S], ACT.Exp, bias=lg[:, n:n + 1]).then_inc(d_exped, 1)
                    act.activation(dec[:, n, S:3 * P], bank[7][:, S:3 * P], ACT.Exp, bias=lg[:, 8 + n:8 + n + 1]).then_inc(d_exped, 1)
                if s in (72, 80):
                    n = (s - 72) // 8
                    act.wait_ge(chunk_used, s)
                    if n == 0:
                        act.wait_ge(padded, 3)
                    for j in range(NJ):
                        act.activation(mv[:, j, 2 * n:2 * n + 2, 0:MV], bank[2 * n + j][:, :].rearrange("p (h d) -> p h d", h=2),
                                       ACT.Copy, scale=r1[:, j:j + 1]).then_inc(evacuated, 1)
                if MP_SLOT < s < MP_SLOT + 2 * MH and (s - MP_SLOT) % 2 == 1:
                    n = (s - MP_SLOT) // 2
                    for j in range(NJ):
                        act.wait_ge(m_summed, 2 * n + j + 1)
                        act.activation(hm[:, j, n, :], bank[4 + 3 * j][:, 0:MV + 1], ACT.Copy).then_inc(m_out, 1)
                if s in (88, 96):
                    n = (s - 88) // 8
                    act.wait_ge(chunk_used, s)
                    if n == 0:
                        act.wait_ge(a_summed, AH)
                    for j in range(NJ):
                        act.activation(o_sig[:, j, COLS * n:COLS * n + COLS], bank[2 * n + j][:, :], ACT.Sigmoid,
                                       scale=r1[:, j:j + 1]).then_inc(evacuated, 1)
                if s == 90:
                    act.wait_ge(m_out, 2 * MH)
                    for j in range(NJ):
                        act.activation(squares[:, 1024 * j:1024 * j + 1024].rearrange("p (h d) -> p h d", h=MH),
                                       hm[:, j, :, 0:MV], ACT.Square).then_inc(m_squared, 1)
                if s == 93:
                    act.wait_ge(m_mean, 1)
                    act.activation(m_ss, m_ss, ACT.Sqrt).then_inc(m_root, 1)
                if s in (100, 101):
                    for n in (2 * (s - 100), 2 * (s - 100) + 1):
                        act.wait_ge(hm_turned, n + 1)
                        for k in range(2):
                            act.activation(t_hi[:, 8 + 2 * n + k, :], bank[4 + n][:, S * k:S * k + S], ACT.Copy,
                                           scale=par[:, C_MN + 2 * n + k:C_MN + 2 * n + k + 1]).then_inc(hm_hi, 1)
                if s in (117, 121, 125, 129):
                    n = (s - 117) // 4
                    act.wait_ge(out_added, 4 + n + 1)
                    for j in range(NJ):
                        if 2 * n + j:
                            act.wait_ge(h_squared, 2 * n + j)
                        act.activation(squares[:, 0:COLS], h[:, j, COLS * n:COLS * n + COLS], ACT.Square,
                                       accum_out=ss2[:, 4 * j + n:4 * j + n + 1]).then_inc(h_squared, 1)
                if s in (119, 123, 127, 131):
                    n = (s - 119) // 4
                    for k in range(4):
                        if k % 2 == 0:
                            act.wait_ge(h_turned, 2 * n + k // 2 + 1)
                        kt = 4 * n + k
                        dst = t_hi[:, kt, :] if kt < 8 else a_hi[:, kt - 8, :]
                        act.activation(dst, bank[4 + 2 * (n % 2) + k // 2][:, S * (k % 2):S * (k % 2) + S], ACT.Copy,
                                       scale=par[:, C_N2 + kt:C_N2 + kt + 1]).then_inc(u2_hi, 1)
                if s == 132:
                    act.wait_ge(h_mean, 1)
                    act.activation(s2sum, s2sum, ACT.Sqrt).then_inc(h_root, 1)
                if s == G0 + 8:
                    act.wait_ge(chunk_used, U0)
                    act.wait_ge(r2_ready, 1)
                    gate_silu(0)
                if s == G1 + 3:
                    ff_part(0)
                if s == G1 + 8:
                    act.wait_ge(chunk_used, U1)
                    gate_silu(1)
                split_at(s + CHUNKS_AHEAD)

            def turn(i, first):
                for rel in range(PER_GROUP):
                    if rel == 9:
                        ff_part(i)
                    if rel == 16:
                        act.wait_ge(chunk_used, first + 16)
                        gate_silu(i + 1)
                    c = rel + CHUNKS_AHEAD
                    split(first + c, i * 48 + (16 * (LOOP0 // 8 + 1) - 48 + 16 * (c // 8)), c % 8)

            with act.Fori(1, GROUPS - 1) as i:
                turn(i, i * PER_GROUP + (LOOP0 - PER_GROUP))
            for s in range(TAIL0, CHUNKS):
                if s == TAIL0 + 8:
                    ff_part(GROUPS - 1)
                split_at(s + CHUNKS_AHEAD)

        @block.tensor
        def _(pe):
            def product(ps, s_hi, s_lo, m_hi, m_lo, start, stop, skip=False):
                pe.matmul(ps, s_hi, m_hi, start=start, stop=False, skip_group_check=skip)
                pe.matmul(ps, s_hi, m_lo, start=False, stop=False, skip_group_check=skip)
                return pe.matmul(ps, s_lo, m_hi, start=False, stop=stop, skip_group_check=skip)

            def tile_of(kt, kind):
                if kind == "u":
                    return t_hi[:, kt, :], t_lo[:, kt, :]
                if kind == "u2":
                    return (t_hi[:, kt, :], t_lo[:, kt, :]) if kt < 8 else (a_hi[:, kt - 8, :], a_lo[:, kt - 8, :])
                if kind == "attention":
                    return a_hi[:, kt, :], a_lo[:, kt, :]
                if kind == "mlstm":
                    return t_hi[:, 8 + kt, :], t_lo[:, 8 + kt, :]
                return ff_hi[:, kt, :], ff_lo[:, kt, :]

            def chunk(c, slot, q, last, pair, kind):
                pe.wait_ge(lo_ready, c + 1)
                for k in range(CHUNK):
                    a_h, a_l = tile_of(CHUNK * q + k, kind)
                    for j in range(NJ):
                        mm = product(bank[pair + j][:, :], a_h[:, j * P:j * P + P], a_l[:, j * P:j * P + P],
                                     w_hi[:, slot, k, :], w_lo[:, slot, k, :],
                                     start=(q == 0 and k == 0), stop=(q == last and k == CHUNK - 1))
                mm.then_inc(chunk_used, 1)

            def chunk_by_channel(c, slot, q, pair):
                pe.wait_ge(lo_ready, c + 1)
                for k in range(CHUNK):
                    kt = CHUNK * q + k
                    for ct in range(4):
                        mm = product(bank[pair + ct // 2][:, S * (ct % 2):S * (ct % 2) + S],
                                     w_hi[:, slot, k, P * ct:P * ct + P], w_lo[:, slot, k, P * ct:P * ct + P],
                                     t_hi[:, kt, :], t_lo[:, kt, :],
                                     start=(kt == 0 and ct % 2 == 0), stop=(kt == KD - 1), skip=True)
                mm.then_inc(chunk_used, 1)

            def turn_x(c):
                if c % 2 == 0:
                    pe.wait_ge(x_landed[c // 2], 16)
                if c >= 4:
                    pe.wait_ge(u_lo, 2 * (c - 4) + 2)
                for k in range(2):
                    for j in range(NJ):
                        kt = 2 * c + k
                        mm = pe.transpose(bank[4 + c % 4][:, S * k + P * j:S * k + P * j + P],
                                          h[:, j, P * kt:P * kt + P], ident)
                mm.then_inc(x_turned, 1)

            def turn_ff(g):
                pe.wait_ge(ff_ready, g + 1)
                for b in range(2):
                    for k in range(2):
                        for j in range(NJ):
                            mm = pe.transpose(bank[2 + b][:, S * k + P * j:S * k + P * j + P],
                                              ff[:, j, P * (2 * b + k):P * (2 * b + k) + P], ident)
                    mm.then_inc(ff_turned, 1)

            pe.wait_ge(con_landed, 16)
            pe.wait_ge(par_landed, 16 * 6)
            pe.transpose(bank[2][:, 0:C_ALL], param_rows, con[0:C_ALL, K_ID:K_ID + C_ALL]).then_inc(par_turned, 1)
            for c in range(4):
                turn_x(c)

            for s in range(LOOP0):
                if 1 <= s <= 4:
                    turn_x(s + 3)
                if s == 9:
                    pe.wait_ge(r1_ready, 1)
                    for j in range(NJ):
                        mm = pe.matmul(bank[7][:, P * j:P * j + P], r1[:, j:j + 1].broadcast_to([P, P]), ident,
                                       start=True, stop=True)
                    mm.then_inc(r_spread, 1)
                if s in (15, 23, 31, 39):
                    b = s // 8 - 1
                    pe.wait_ge(roped, b + 1)
                    if b:
                        pe.wait_ge(qk_out, 2 * b)
                    for n in range(2):
                        for k in range(2):
                            for j in range(NJ):
                                mm = pe.transpose(bank[4 + n][:, S * k + P * j:S * k + P * j + P],
                                                  rot[:, j, 2 * n + k, :], ident)
                        mm.then_inc(qk_turned, 1)
                if s >= NHEAD_SLOT + 5 and (s - NHEAD_SLOT) % 3 == 2 and (s - NHEAD_SLOT - 5) // 3 < AH:
                    n = (s - NHEAD_SLOT - 5) // 3
                    pe.wait_ge(a_weighted, n + 1)
                    pe.wait_ge(evacuated, 10 if n < 4 else 12)
                    if n:
                        pe.wait_ge(a_out, n)
                    pe.matmul(bank[6][:, 0:AD + 1], p_t[:, 0:P], v_tok[:, 0, n, :], start=True, stop=True)
                    pe.matmul(bank[6][:, AD + 1:2 * AD + 2], p_t[:, P:2 * P], v_tok[:, 0, n, :], start=True, stop=False)
                    pe.matmul(bank[6][:, AD + 1:2 * AD + 2], p_t[:, 2 * P:3 * P], v_tok[:, 1, n, :],
                              start=False, stop=True).then_inc(a_summed, 1)
                if s >= NHEAD_SLOT + 3 and (s - NHEAD_SLOT) % 3 == 0 and (s - NHEAD_SLOT - 3) // 3 < AH:
                    n = (s - NHEAD_SLOT - 3) // 3
                    pe.wait_ge(a_exped, 2 * n + 2)
                    if n:
                        pe.wait_ge(a_weighted, n)
                    else:
                        pe.wait_ge(qk_out, 8)
                    for k in range(3):
                        mm = pe.transpose(bank[5][:, P * k:P * k + P], sc[:, n % 2, P * k:P * k + P], ident)
                    mm.then_inc(a_turned, 1)
                if s >= NHEAD_SLOT and (s - NHEAD_SLOT) % 3 == 0 and (s - NHEAD_SLOT) // 3 < AH:
                    n = (s - NHEAD_SLOT) // 3
                    if n == 0:
                        pe.wait_ge(qk_out, 8)
                    else:
                        pe.wait_ge(a_masked, n)
                    pe.matmul(bank[4][:, 0:P], q_t[:, n, 0:P], k_t[:, n, 0:P], start=True, stop=True)
                    pe.matmul(bank[4][:, P:3 * P], q_t[:, n, P:S], k_t[:, n, :], start=True, stop=True).then_inc(a_scored, 1)
                if s in (76, 79):
                    n = (s - 76) // 3
                    pe.wait_ge(a_normed, 2)
                    if n:
                        pe.wait_ge(ha_lo, 4)
                    for b in range(2):
                        for k in range(2):
                            for j in range(NJ):
                                mm = pe.transpose(bank[5 + b][:, S * k + P * j:S * k + P * j + P],
                                                  ha[:, j, 4 * n + 2 * b + k, 0:AD], ident)
                        mm.then_inc(ha_turned, 1)
                if s == 48:
                    pe.wait_ge(wg_lo_ready, 1)
                    pe.wait_ge(r_row_ready, 1)
                    for j in range(NJ):
                        for kt in range(KD):
                            mm = product(bank[7][:, 8 * j:8 * j + 8], t_hi[:, kt, P * j:P * j + P], t_lo[:, kt, P * j:P * j + P],
                                         wg_hi[:, kt, :], wg_lo[:, kt, :], start=(kt == 0), stop=(kt == KD - 1))
                    mm.then_inc(g_summed, 1)
                if s == 56:
                    pe.wait_ge(g_logf, 1)
                    for j in range(NJ):
                        pe.transpose(bank[7][0:MH, P * j:P * j + P], lf[:, MH * j:MH * j + MH], ident)
                        mm = pe.transpose(bank[7][0:MH, S + P * j:S + P * j + P], lg[:, 8 * j:8 * j + MH], ident)
                    mm.then_inc(g_turned, 1)
                if s == 59:
                    pe.wait_ge(m_scanned, 2)
                    for j in range(NJ):
                        mm = pe.transpose(bank[7][:, MH * j:MH * j + MH], m_row[:, 0, P * j:P * j + P], con[0:MH, K_ID:K_ID + MH])
                    mm.then_inc(m_turned, 1)
                if DEC_SLOT <= s < DEC_SLOT + 2 * MH and (s - DEC_SLOT) % 2 == 0:
                    n = (s - DEC_SLOT) // 2
                    pe.wait_ge(seg_ready, 2 * MH)
                    if n == 0:
                        pe.wait_ge(m_exped, 1)
                    else:
                        pe.wait_ge(d_exped, 2 * n)
                    pick = con[0:MH, K_ID + n:K_ID + n + 1].broadcast_to([MH, P])
                    for j, ps in ((0, bank[7][:, 0:P]), (1, bank[7][:, 2 * P:3 * P])):
                        pe.matmul(ps, seg[:, j, n, :], upper, start=True, stop=False)
                        pe.matmul(ps, ident, con[:, K_NU:K_NU + P], start=False, stop=False)
                        mm = pe.matmul(ps, pick, m_row[:, 1, P * j:P * j + P], start=False, stop=True)
                    ps = bank[7][:, P:2 * P]
                    pe.matmul(ps, seg[:, 0, n, :], one.broadcast_to([P, P]), start=True, stop=False)
                    pe.matmul(ps, lf[:, MH + n:MH + n + 1].broadcast_to([P, P]), upper, start=False, stop=False)
                    pe.matmul(ps, pick, m_row[:, 1, P:S], start=False, stop=True).then_inc(d_summed, 1)
                if MS_SLOT <= s < MS_SLOT + 2 * MH and (s - MS_SLOT) % 2 == 0:
                    n = (s - MS_SLOT) // 2
                    if n == 0:
                        pe.wait_ge(d_exped, 2 * MH)
                        pe.wait_ge(conv_silu, 2)
                    else:
                        pe.wait_ge(m_decayed, n)
                    pe.matmul(bank[7][:, 0:S], mqk[:, 4 + n, 0:P], mqk[:, n, :], start=True, stop=True)
                    pe.matmul(bank[7][:, S:3 * P], mqk[:, 4 + n, P:S], mqk[:, n, P:S], start=True, stop=True).then_inc(m_scored, 1)
                if MP_SLOT <= s < MP_SLOT + 2 * MH and (s - MP_SLOT) % 2 == 0:
                    n = (s - MP_SLOT) // 2
                    pe.wait_ge(m_decayed, MH)
                    pe.wait_ge(evacuated, 16 if n >= 2 else 14)
                    if n:
                        pe.wait_ge(m_out, 2 * n)
                    pe.matmul(bank[4][:, 0:MV + 1], dec[:, n, 0:P], mv[:, 0, n, :], start=True, stop=True).then_inc(m_summed, 1)
                    pe.matmul(bank[7][:, 0:MV + 1], dec[:, n, P:S], mv[:, 0, n, :], start=True, stop=False)
                    pe.matmul(bank[7][:, 0:MV + 1], dec[:, n, S:3 * P], mv[:, 1, n, :], start=False, stop=True).then_inc(m_summed, 1)
                if s == 99:
                    pe.wait_ge(m_normed, 2 * MH)
                    pe.wait_ge(ha_lo, 8)
                    for n in range(MH):
                        for k in range(2):
                            for j in range(NJ):
                                mm = pe.transpose(bank[4 + n][:, S * k + P * j:S * k + P * j + P],
                                                  hm[:, j, n, P * k:P * k + P], ident)
                        mm.then_inc(hm_turned, 1)
                if s in (118, 122, 126, 130):
                    n = (s - 118) // 4
                    pe.wait_ge(out_added, 4 + n + 1)
                    if n < 2:
                        pe.wait_ge(hm_lo, 8)
                    else:
                        pe.wait_ge(u2_lo, 4 * (n - 1))
                    for b in range(2):
                        for k in range(2):
                            for j in range(NJ):
                                kt = 4 * n + 2 * b + k
                                mm = pe.transpose(bank[4 + 2 * (n % 2) + b][:, S * k + P * j:S * k + P * j + P],
                                                  h[:, j, P * kt:P * kt + P], ident)
                        mm.then_inc(h_turned, 1)
                if s == G1 + 2:
                    turn_ff(0)

                if s < OUT0:
                    b, q = s // IN_CH, s % IN_CH
                    if b == 0:
                        pe.wait_ge(u_lo, 2 * q + 2)
                    if q == 0 and b >= 2:
                        if b < 8:
                            pe.wait_ge(evacuated, 2 * (b - 1))
                        elif b in (8, 9):
                            pe.wait_ge(conv_x_ready, 2 * (b - 7))
                        else:
                            pe.wait_ge(evacuated, 12 + 2 * (b - 9))
                    if q == 0 and b == 1:
                        pe.wait_ge(par_ready, 1)
                    if b in (6, 7):
                        chunk_by_channel(s, s % 4, q, 2 * (b % 2))
                    else:
                        chunk(s, s % 4, q, IN_CH - 1, 2 * (b % 2), "u")
                elif s < FFN0:
                    m, q = (s - OUT0) // OUT_CH, (s - OUT0) % OUT_CH
                    if q == 0:
                        if m < 2:
                            pe.wait_ge(evacuated, 18 + 2 * m)
                        else:
                            pe.wait_ge(out_added, m - 1)
                        pe.wait_ge(ha_lo, 8)
                        if m == NB:
                            pe.wait_ge(hm_lo, 8)
                    chunk(s, s % 4, q, OUT_CH - 1, 2 * (m % 2), "attention" if m < NB else "mlstm")
                else:
                    m, q = (s - FFN0) // IN_CH, (s - FFN0) % IN_CH
                    if m == 0:
                        if q == 0:
                            pe.wait_ge(out_added, 7)
                        pe.wait_ge(u2_lo, 4 * (q // 2) + 4)
                    if m == 1 and q == 0:
                        pe.wait_ge(out_added, 8)
                    if m == 2 and q == 0:
                        pe.wait_ge(gated, 2)
                    if m == 3 and q == 0:
                        pe.wait_ge(ff_lo_ready, 2)
                    chunk(s, s % 4, q, IN_CH - 1, 2 * (m % 2), "u2")

            def down(g, first):
                pe.wait_ge(ff_lo_ready, g * 2 + 2)
                for n in range(NB):
                    if not isinstance(g, int) or g:
                        pe.wait_ge(down_added, g * NB + n - 1)
                    elif n >= 2:
                        pe.wait_ge(down_added, n - 1)
                    for q in range(2):
                        chunk(first + (2 * n + q), (2 * n + q) % 4, q, 1, 4 + 2 * (n % 2), "hidden")

            def turn(i, first):
                down(i - 1, first)
                turn_ff(i)
                pe.wait_ge(gated, i * 2 + 2)
                for q in range(IN_CH):
                    chunk(first + (IN_CH + q), q % 4, q, IN_CH - 1, 0, "u2")
                pe.wait_ge(ff_lo_ready, i * 2 + 2)
                for q in range(IN_CH):
                    chunk(first + (2 * IN_CH + q), q % 4, q, IN_CH - 1, 2, "u2")

            turn(1, LOOP0)
            with pe.Fori(2, GROUPS - 1) as i:
                turn(i, i * PER_GROUP + (LOOP0 - PER_GROUP))
            down(GROUPS - 2, TAIL0)
            turn_ff(GROUPS - 1)
            down(GROUPS - 1, TAIL0 + IN_CH)

        @block.vector
        def _(dve):
            steps = [0]

            def settle(ins):
                steps[0] += 1
                ins.then_inc(settled, 1)
                dve.wait_ge(settled, steps[0])

            def split(c, slot):
                dve.wait_ge(hi_ready, c + 1)
                dve.tensor_tensor(w_lo[:, slot % 4, :, :], raw[:, slot // 2, 2 * (slot % 2):2 * (slot % 2) + 2, :],
                                  w_hi[:, slot % 4, :, :].bitcast(F32), ALU.subtract).then_inc(lo_ready, 1)

            def split_at(c):
                if c < CHUNKS:
                    split(c, c % 8)

            def low_part(dst, ps, scale, hi):
                return dve.scalar_tensor_tensor(out=dst, in0=ps, scalar=scale, in1=hi.bitcast(F32),
                                                op0=ALU.mult, op1=ALU.subtract)

            def u_part(c):
                for k in range(2):
                    kt = 2 * c + k
                    dve.wait_ge(u_hi, 2 * c + 2)
                    low_part(t_lo[:, kt, :], bank[4 + c % 4][:, S * k:S * k + S], par[:, C_N1 + kt:C_N1 + kt + 1],
                             t_hi[:, kt, :]).then_inc(u_lo, 1)

            def ff_part(g):
                for b in range(2):
                    dve.wait_ge(ff_hi_ready, g * 2 + b + 1)
                    dve.tensor_tensor(ff_lo[:, 2 * b:2 * b + 2, :], bank[2 + b][:, :].rearrange("p (k t) -> p k t", k=2),
                                      ff_hi[:, 2 * b:2 * b + 2, :].bitcast(F32), ALU.subtract).then_inc(ff_lo_ready, 1)

            def hidden(g):
                dve.wait_ge(gated, g * 2 + 2)
                for j in range(NJ):
                    mm = dve.scalar_tensor_tensor(out=ff[:, j, :], in0=bank[2 + j][:, :], scalar=r2[:, j:j + 1],
                                                  in1=g_act[:, j, :], op0=ALU.mult, op1=ALU.mult)
                mm.then_inc(ff_ready, 1)

            def add_block(n, pair, signal):
                for j in range(NJ):
                    hb = h[:, j, COLS * n:COLS * n + COLS]
                    mm = dve.tensor_tensor(hb, bank[pair + j][:, :], hb, ALU.add)
                mm.then_inc(signal, 1)

            def rope_table(n):
                for k, (w0, base) in enumerate(((0, K_COS), (64, K_SIN), (64, K_COS), (0, K_SIN))):
                    mm = dve.tensor_tensor(rope_w[:, k, :, :], con[:, base:base + 128].rearrange("p (j d) -> p j d", j=NJ),
                                           qk_w[:, n:n + 1, w0:w0 + 64].broadcast_to([P, NJ, 64]), ALU.mult)
                settle(mm)

            def mean_of(dst, src, n):
                return dve.tensor_scalar(dst, src, 1.0 / n, EPS, ALU.mult, ALU.add)

            dve.wait_ge(con_landed, 16)
            dve.wait_ge(side_landed, 16 * 5)
            rope_table(0)
            dve.wait_ge(par_ready, 1)
            for c in range(CHUNKS_AHEAD):
                u_part(c)
                split_at(c)
            for s in range(LOOP0):
                if s < 4:
                    u_part(s + 4)
                if s == 5:
                    dve.wait_ge(x_squared, 2)
                    mean_of(ss1, ss1, D).then_inc(x_mean, 1)
                if s == 6:
                    dve.wait_ge(x_root, 1)
                    dve.reciprocal(r1, ss1).then_inc(r1_ready, 1)
                if s == 8:
                    dve.wait_ge(wg_hi_ready, 1)
                    dve.tensor_tensor(wg_lo[:, :, :], wg_raw[:, :, :], wg_hi[:, :, :].bitcast(F32),
                                      ALU.subtract).then_inc(wg_lo_ready, 1)
                if s == 10:
                    dve.wait_ge(r_spread, 1)
                    dve.tensor_copy(r_row[:, :], bank[7][:, 0:S]).then_inc(r_row_ready, 1)
                if s == 24:
                    dve.wait_ge(roped, 2)
                    rope_table(1)
                if s in (10, 18, 26, 34):
                    b = s // 8 - 1
                    dve.wait_ge(qk_squared, b + 1)
                    settle(dve.tensor_reduce(qss, sq.rearrange("p j h d -> p (j h) d"), AX.X, ALU.add))
                    mean_of(qss, qss, AD).then_inc(qk_mean, 1)
                if s in (12, 20, 28, 36):
                    b = s // 8 - 1
                    dve.wait_ge(qk_root, b + 1)
                    settle(dve.reciprocal(qss, qss))
                    t3 = tok.rearrange("p j h d -> p (j h) d")
                    settle(dve.tensor_tensor(t3, t3, qss.unsqueeze(2).broadcast_to([P, 8, AD]), ALU.mult))
                if s in (13, 21, 29, 37):
                    b = s // 8 - 1
                    if b:
                        dve.wait_ge(qk_turned, 2 * b)
                    def wide(k):
                        return rope_w[:, k, :, :].unsqueeze(2).broadcast_to([P, NJ, 4, 64])
                    dve.tensor_tensor(rope_a, tok[:, :, :, 0:64], wide(0), ALU.mult)
                    settle(dve.tensor_tensor(rope_b, tok[:, :, :, 64:128], wide(1), ALU.mult))
                    settle(dve.tensor_tensor(rot[:, :, :, 0:64], rope_a, rope_b, ALU.subtract))
                if s in (14, 22, 30, 38):
                    dve.tensor_tensor(rope_a, tok[:, :, :, 64:128], wide(2), ALU.mult)
                    settle(dve.tensor_tensor(rope_b, tok[:, :, :, 0:64], wide(3), ALU.mult))
                    dve.tensor_tensor(rot[:, :, :, 64:128], rope_a, rope_b, ALU.add).then_inc(roped, 1)
                if s == 41:
                    dve.wait_ge(roped, 4)
                    settle(dve.memset(conv_x[:, :, 0:3], 0.0))
                if s >= NHEAD_SLOT + 4 and (s - NHEAD_SLOT) % 3 == 1 and (s - NHEAD_SLOT - 4) // 3 < AH:
                    n = (s - NHEAD_SLOT - 4) // 3
                    dve.wait_ge(a_turned, n + 1)
                    if n:
                        dve.wait_ge(a_summed, n)
                    dve.tensor_tensor(p_t[:, :], bank[5][:, 0:3 * P], con[:, K_W:K_W + 3 * P], ALU.mult).then_inc(a_weighted, 1)
                if s >= NHEAD_SLOT + 1 and (s - NHEAD_SLOT) % 3 == 1 and (s - NHEAD_SLOT - 1) // 3 < AH:
                    n = (s - NHEAD_SLOT - 1) // 3
                    m = n % 2
                    dve.wait_ge(a_scored, n + 1)
                    if n >= 2:
                        dve.wait_ge(a_turned, n - 1)
                    dve.tensor_tensor_reduce(sc[:, m, 0:P], bank[4][:, 0:P], con[:, K_NEG + P:K_NEG + 2 * P], AD ** -0.5,
                                             -3.0e38, ALU.add, ALU.max, a_max[:, 2 * m:2 * m + 1])
                    settle(dve.tensor_tensor_reduce(sc[:, m, P:3 * P], bank[4][:, P:3 * P], con[:, K_NEG:K_NEG + 2 * P],
                                                    AD ** -0.5, -3.0e38, ALU.add, ALU.max, a_max[:, 2 * m + 1:2 * m + 2]))
                    dve.tensor_scalar(a_neg[:, 2 * m:2 * m + 2], a_max[:, 2 * m:2 * m + 2], -1.0, None,
                                      ALU.mult).then_inc(a_masked, 1)
                if s == 71:
                    dve.wait_ge(a_squared, 2)
                    dve.tensor_reduce(a_ss, ha_sq.rearrange("p j h d -> p (j h) d"), AX.X, ALU.add)
                    settle(dve.reciprocal(a_rd, ha[:, :, :, AD]))
                    settle(dve.tensor_tensor(a_ss, a_ss, a_rd, ALU.mult))
                    settle(dve.tensor_tensor(a_ss, a_ss, a_rd, ALU.mult))
                    mean_of(a_ss, a_ss, AD).then_inc(a_mean, 1)
                if s == 74:
                    dve.wait_ge(a_root, 1)
                    settle(dve.reciprocal(a_r, a_ss))
                    settle(dve.tensor_tensor(a_r, a_r, a_rd, ALU.mult))
                    for j in range(NJ):
                        dve.tensor_tensor(ha[:, j, :, 0:AD], ha[:, j, :, 0:AD],
                                          a_r[:, AH * j:AH * j + AH].unsqueeze(2).broadcast_to([P, AH, AD]),
                                          ALU.mult).then_inc(a_normed, 1)
                if s in (78, 81):
                    n = (s - 78) // 3
                    for k in range(4):
                        ch = 4 * n + k
                        dve.wait_ge(ha_hi, 4 * n + 2 * (k // 2) + 2)
                        low_part(a_lo[:, ch, :], bank[5 + k // 2][:, S * (k % 2):S * (k % 2) + S],
                                 par[:, C_AN + ch:C_AN + ch + 1], a_hi[:, ch, :]).then_inc(ha_lo, 1)
                if s == 49:
                    dve.wait_ge(g_summed, 1)
                    for j in range(NJ):
                        dve.scalar_tensor_tensor(out=z[:, 8 * j:8 * j + 8], in0=bank[7][:, 8 * j:8 * j + 8],
                                                 scalar=r1[:, j:j + 1], in1=gate_b[:, :], op0=ALU.mult,
                                                 op1=ALU.add).then_inc(g_z, 1)
                if s == 51:
                    dve.wait_ge(g_tanh, 1)
                    dve.tensor_scalar(lg, z, GATE_CAP, None, ALU.mult).then_inc(g_capped, 1)
                if s == 53:
                    dve.wait_ge(g_exped, 1)
                    settle(dve.tensor_scalar(u_f, e_f, 1.0, None, ALU.add))
                    dve.tensor_scalar(c_f, u_f, -1.0, None, ALU.add).then_inc(g_plus1, 1)
                    settle(dve.reciprocal(ru_f, u_f))
                    settle(dve.tensor_tensor(c_f, e_f, c_f, ALU.subtract))
                    settle(dve.tensor_tensor(c_f, c_f, ru_f, ALU.mult))
                if s == 55:
                    dve.wait_ge(g_logged, 1)
                    settle(dve.tensor_tensor(lf, ln_f, c_f, ALU.add))
                    dve.tensor_scalar(lf, lf, -1.0, None, ALU.mult).then_inc(g_logf, 1)
                if s == 58:
                    dve.wait_ge(g_rows, 1)
                    dve.tensor_tensor_scan(m_row[:, 0, :], g_row[:, 0, :], g_row[:, 1, :], 0.0, ALU.add, ALU.max
                                           ).then_inc(m_scanned, 1)
                    dve.wait_ge(m_scanned, 1)
                    dve.tensor_scalar(m_row[:, 1, :], m_row[:, 0, :], -1.0, None, ALU.mult).then_inc(m_scanned, 1)
                    dve.wait_ge(g_logf, 1)
                    for j in range(NJ):
                        for n in range(MH):
                            dve.tensor_scalar(seg[:, j, n, :], con[:, K_L:K_L + P], lf[:, MH * j + n:MH * j + n + 1], None,
                                              ALU.mult).then_inc(seg_ready, 1)
                if s in (56, 64):
                    n = (s - 56) // 8
                    dve.wait_ge(chunk_used, s)
                    for b in range(2):
                        dve.tensor_tensor(conv_x[:, 2 * b:2 * b + 2, 3:3 + S],
                                          bank[2 * n + b][:, :].rearrange("p (c t) -> p c t", c=2),
                                          r_row[:, :].unsqueeze(1).broadcast_to([P, 2, S]), ALU.mult).then_inc(conv_x_ready, 1)
                if 57 <= s <= 60 or 65 <= s <= 68:
                    n, ct = (s - 57) // 8, (s - 57) % 8
                    ch = 4 * n + ct
                    dve.wait_ge(conv_x_ready, 2 * n + 2)
                    settle(dve.tensor_scalar(mqk[:, ch, :], conv_x[:, ct, 0:S], par[:, C_CW + ch:C_CW + ch + 1],
                                             par[:, C_CB + ch:C_CB + ch + 1], ALU.mult, ALU.add))
                    for t in range(1, 4):
                        mm = dve.scalar_tensor_tensor(out=mqk[:, ch, :], in0=conv_x[:, ct, t:t + S],
                                                      scalar=par[:, C_CW + 8 * t + ch:C_CW + 8 * t + ch + 1],
                                                      in1=mqk[:, ch, :], op0=ALU.mult, op1=ALU.add)
                        if t < 3:
                            settle(mm)
                    mm.then_inc(conv_done, 1)
                if MS_SLOT < s < MS_SLOT + 2 * MH and (s - MS_SLOT) % 2 == 1:
                    n = (s - MS_SLOT) // 2
                    dve.wait_ge(m_scored, n + 1)
                    dve.scalar_tensor_tensor(out=dec[:, n, :], in0=bank[7][:, 0:3 * P], scalar=MQ ** -0.5, in1=dec[:, n, :],
                                             op0=ALU.mult, op1=ALU.mult).then_inc(m_decayed, 1)
                if s == 65:
                    dve.wait_ge(a_scored, AH)
                    dve.memset(mv[:, :, :, MV:MV + 1], 1.0).then_inc(padded, 1)
                if s == 91:
                    dve.wait_ge(m_squared, 2)
                    dve.wait_ge(m_exped, 1)
                    m3 = m_den.rearrange("p (j h) -> p j h", j=NJ)
                    dve.tensor_reduce(m_ss, squares.rearrange("p (k d) -> p k d", d=MV), AX.X, ALU.add)
                    settle(dve.tensor_scalar(m3, hm[:, :, :, MV], -1.0, None, ALU.mult))
                    settle(dve.tensor_tensor(m3, m3, hm[:, :, :, MV], ALU.max))
                    settle(dve.tensor_tensor(m_den, m_den, m_exp, ALU.max))
                    settle(dve.reciprocal(m_rd, m_den))
                    settle(dve.tensor_tensor(m_ss, m_ss, m_rd, ALU.mult))
                    settle(dve.tensor_tensor(m_ss, m_ss, m_rd, ALU.mult))
                    mean_of(m_ss, m_ss, MV).then_inc(m_mean, 1)
                if s == 94:
                    dve.wait_ge(m_root, 1)
                    settle(dve.reciprocal(m_r, m_ss))
                    settle(dve.tensor_tensor(m_r, m_r, m_rd, ALU.mult))
                if s in (97, 98):
                    j = s - 97
                    dve.wait_ge(evacuated, 20)
                    for n in range(MH):
                        dve.scalar_tensor_tensor(out=hm[:, j, n, 0:MV], in0=hm[:, j, n, 0:MV],
                                                 scalar=m_r[:, MH * j + n:MH * j + n + 1],
                                                 in1=o_sig[:, j, MV * n:MV * n + MV], op0=ALU.mult, op1=ALU.mult
                                                 ).then_inc(m_normed, 1)
                if s in (101, 102):
                    for n in (2 * (s - 101), 2 * (s - 101) + 1):
                        dve.wait_ge(hm_hi, 2 * n + 2)
                        for k in range(2):
                            kt = 2 * n + k
                            low_part(t_lo[:, 8 + kt, :], bank[4 + n][:, S * k:S * k + S], par[:, C_MN + kt:C_MN + kt + 1],
                                     t_hi[:, 8 + kt, :]).then_inc(hm_lo, 1)
                if OUT0 + 4 <= s <= FFN0 and s % 4 == 0:
                    m = (s - OUT0) // 4 - 1
                    dve.wait_ge(chunk_used, s)
                    if m == 0:
                        dve.wait_ge(x_squared, 2)
                    if m >= NB:
                        dve.wait_ge(out_added, m - NB + 1)
                    add_block(m % NB, 2 * (m % 2), out_added)
                if s in (120, 124, 128, 132):
                    n = (s - 120) // 4
                    for k in range(4):
                        kt = 4 * n + k
                        dve.wait_ge(u2_hi, 4 * n + 2 * (k // 2) + 2)
                        d_hi, d_lo = (t_hi[:, kt, :], t_lo[:, kt, :]) if kt < 8 else (a_hi[:, kt - 8, :], a_lo[:, kt - 8, :])
                        low_part(d_lo, bank[4 + 2 * (n % 2) + k // 2][:, S * (k % 2):S * (k % 2) + S],
                                 par[:, C_N2 + kt:C_N2 + kt + 1], d_hi).then_inc(u2_lo, 1)
                if s == 131:
                    dve.wait_ge(h_squared, 8)
                    settle(dve.tensor_reduce(s2sum, ss2.rearrange("p (j n) -> p j n", j=NJ), AX.X, ALU.add))
                    mean_of(s2sum, s2sum, D).then_inc(h_mean, 1)
                if s == 133:
                    dve.wait_ge(h_root, 1)
                    dve.reciprocal(r2, s2sum).then_inc(r2_ready, 1)
                if s == U0 + 8:
                    dve.wait_ge(chunk_used, G1)
                    dve.wait_ge(r2_ready, 1)
                    hidden(0)
                if s == G1 + 4:
                    ff_part(0)
                split_at(s + CHUNKS_AHEAD)

            def turn(i, first, tail=False):
                dve.wait_ge(chunk_used, first)
                dve.wait_ge(ff_turned, i * 2)
                hidden(i)
                for rel in range(PER_GROUP):
                    if rel in (2, 4, 6, 8):
                        n = rel // 2 - 1
                        dve.wait_ge(chunk_used, first + rel)
                        dve.wait_ge(out_added, 2 * NB)
                        if not isinstance(i, int) or i > 1:
                            dve.wait_ge(down_added, i * NB + (n + 1 - 2 * NB))
                        add_block(n, 4 + 2 * (n % 2), down_added)
                    if rel == 10:
                        ff_part(i)
                    c = rel + CHUNKS_AHEAD
                    split(first + c, c % 8)

            turn(1, LOOP0)
            with dve.Fori(2, GROUPS - 1) as i:
                turn(i, i * PER_GROUP + (LOOP0 - PER_GROUP))
            for s in range(TAIL0, CHUNKS + 1):
                rel = s - TAIL0
                if rel == 0:
                    dve.wait_ge(chunk_used, s)
                    dve.wait_ge(ff_turned, 2 * (GROUPS - 1))
                    hidden(GROUPS - 1)
                if rel == 8:
                    ff_part(GROUPS - 1)
                if rel >= 2 and rel % 2 == 0:
                    m = NB * (GROUPS - 2) + rel // 2 - 1
                    dve.wait_ge(chunk_used, s)
                    dve.wait_ge(down_added, m + 1 - NB)
                    add_block(m % NB, 4 + 2 * (m % 2), down_added)
                split_at(s + CHUNKS_AHEAD)


_NAMES = ["x", "norm1_w", "w_in", "conv_w", "conv_b", "igate_b", "fgate_b", "q_norm_w", "k_norm_w",
          "mlstm_norm_w", "attn_norm_w", "w_out", "norm2_w", "w_gate", "w_up", "w_down"]


def kernel(**inputs):
    import concourse.bacc as bacc
    from concourse.bass_utils import run_bass_kernel_spmd

    nc = bacc.Bacc("TRN2", target_bir_lowering=False, num_devices=1)
    arrays = {name: np.ascontiguousarray(inputs[name]) for name in _NAMES}
    arrays["shape_consts"] = constants()
    args = [nc.dram_tensor(name, a.shape, mybir.dt.from_np(a.dtype), kind="ExternalInput").ap()
            for name, a in arrays.items()]
    out = nc.dram_tensor("out", (1, S, D), F32, kind="ExternalOutput").ap()
    build(nc, *args, out)
    return run_bass_kernel_spmd(nc, [arrays], core_ids=[0]).results[0]["out"]
```

```python
from contextlib import ExitStack

import numpy as np
import concourse.bass as bass
from concourse import mybir

F32 = mybir.dt.float32
F32R = mybir.dt.float32r
ALU = mybir.AluOpType
ACT = mybir.ActivationFunctionType
AX = mybir.AxisListType

P = 128
D = 2048
S = 256
NJ = S // P
KD = D // P
MH, MQ, MV = 4, 128, 256
AH, AD = 8, 128
GATE_CAP = 15.0
EPS = 1e-6
FF = 5632
COLS = 512
PIECE = 4
CHUNK = 2
PIECES = 4
CHUNKS_AHEAD = 4
LEAD = 3
OFF_MQ, OFF_MK, OFF_MV, OFF_MO, OFF_GATES = 0, 512, 1024, 2048, 3072
OFF_AQ, OFF_AK, OFF_AV = 3080, 4104, 5128
IN_BLOCKS = [OFF_AQ, OFF_AQ + COLS, OFF_AK, OFF_AK + COLS, OFF_AV, OFF_AV + COLS,
             OFF_MQ, OFF_MK, OFF_MV, OFF_MV + COLS, OFF_MO, OFF_MO + COLS]
IN_CH = KD // CHUNK
OUT0 = len(IN_BLOCKS) * IN_CH
OUT_CH = KD // 2 // CHUNK
NB = D // COLS
OUT1 = OUT0 + NB * OUT_CH
FFN0 = OUT1 + NB * OUT_CH
GROUPS = FF // COLS
TURNS = 16
G0, U0, G1, U1 = (FFN0 + IN_CH * n for n in range(4))
LOOP0 = FFN0 + 4 * IN_CH
PER_GROUP = 3 * IN_CH
TAIL0 = LOOP0 + PER_GROUP * (GROUPS - 2)
CHUNKS = TAIL0 + 2 * IN_CH
C_N1, C_AN, C_MN, C_N2, C_CW, C_CB, C_ALL = 0, 16, 24, 32, 48, 80, 88
K_ID, K_COS, K_SIN, K_NEG, K_W, K_L, K_U, K_NU, K_ALL = 0, 128, 256, 384, 640, 1024, 1152, 1280, 1408
NEG = -1e30
X_PARTS = [0, 256, 512, 1024, 1536, 2048]
NHEAD_SLOT = 44
DEC_SLOT = 62
MS_SLOT = 71
MP_SLOT = 82


def constants():
    c = np.zeros((P, K_ALL), np.float32)
    r = np.arange(P)
    c[:, K_ID:K_COS] = np.eye(P)
    inv = (np.float32(10000.0) ** (-np.arange(0, AD, 2, dtype=np.float32) / np.float32(AD))).astype(np.float32)
    ang = np.arange(S, dtype=np.float32)[:, None] * inv[None, :]
    for j in range(NJ):
        a = ang[j * P:(j + 1) * P].astype(np.float64)
        c[:, K_COS + 64 * j:K_COS + 64 * j + 64] = np.cos(a)
        c[:, K_SIN + 64 * j:K_SIN + 64 * j + 64] = np.sin(a)
    t, s = np.arange(S)[:, None], np.arange(S)[None, :]
    d = t - s
    seen = ((d >= 0) & (d <= 128)) * 1 + ((d >= 0) & (d % 4 == 0)) * 1 + ((d >= 0) & (d % 16 == 0)) * 1
    c[:, K_NEG:K_W] = np.where(seen[P:] > 0, 0.0, NEG)
    c[:, K_W:K_W + P] = seen[:P, :P].T
    c[:, K_W + P:K_W + 2 * P] = seen[P:, :P].T
    c[:, K_W + 2 * P:K_W + 3 * P] = seen[P:, P:].T
    c[:, K_L:K_U] = r[:, None] > r[None, :]
    c[:, K_U:K_NU] = r[:, None] <= r[None, :]
    c[:, K_NU:K_ALL] = np.where(r[:, None] > r[None, :], NEG, 0.0)
    return c


def build(nc, x, norm1_w, w_in, conv_w, conv_b, igate_b, fgate_b, q_norm_w, k_norm_w,
          mlstm_norm_w, attn_norm_w, w_out, norm2_w, w_gate, w_up, w_down, consts, out):
    with ExitStack() as ctx:
        def sb(name, shape, dt=F32):
            return ctx.enter_context(nc.sbuf_tensor(name, shape, dt))

        def sem(name):
            return ctx.enter_context(nc.semaphore(name))

        h = sb("h", [P, NJ, D])
        raw = sb("raw", [P, PIECES, PIECE, COLS])
        w_hi = sb("w_hi", [P, CHUNKS_AHEAD, CHUNK, COLS], F32R)
        w_lo = sb("w_lo", [P, CHUNKS_AHEAD, CHUNK, COLS], F32R)
        t_hi = sb("t_hi", [P, KD, S], F32R)
        t_lo = sb("t_lo", [P, KD, S], F32R)
        a_hi = sb("a_hi", [P, KD // 2, S], F32R)
        a_lo = sb("a_lo", [P, KD // 2, S], F32R)
        ff_hi = sb("ff_hi", [P, PIECE, S], F32R)
        ff_lo = sb("ff_lo", [P, PIECE, S], F32R)
        con = sb("con", [P, K_ALL])
        par = sb("par", [P, C_ALL])
        qk_w = sb("qk_w", [P, 2, AD])
        rope_w = sb("rope_w", [P, 4, NJ, 64])
        wg = sb("wg", [P, KD * 16 + P - 16], F32R)
        gate_b = sb("gate_b", [P, 8])
        area1 = sb("area1", [P, 3584])
        area2 = sb("area2", [P, 2 * NJ * MH * (MV + 1)])
        v_tok = sb("v_tok", [P, NJ, AH, AD + 1])
        ha = sb("ha", [P, NJ, AH, AD + 1])
        seg = sb("seg", [P, NJ, MH, P])
        area6 = sb("area6", [P, 4 * (S + 3)])
        sc = sb("sc", [P, 2, 3 * P])
        p_t = sb("p_t", [P, 3 * P])
        small = sb("small", [P, 256])
        r_row = sb("r_row", [P, S])

        tok = area1[:, 0:1024].rearrange("p (j h d) -> p j h d", j=NJ, h=4)
        rot = area1[:, 1024:2048].rearrange("p (j h d) -> p j h d", j=NJ, h=4)
        sq = area1[:, 2048:3072].rearrange("p (j h d) -> p j h d", j=NJ, h=4)
        norm1_rows = area1[0:C_AN, 3072:3200]
        param_rows = area1[0:C_ALL - C_AN, 3200:3328]
        squares = area1[:, 0:2048]
        mqk = area1[:, 0:2048].rearrange("p (h t) -> p h t", h=8)
        dec = area1[:, 2048:3584].rearrange("p (h t) -> p h t", h=MH)
        g_act = area1[:, 0:1024].rearrange("p (j c) -> p j c", j=NJ)
        ff = area1[:, 1024:2048].rearrange("p (j c) -> p j c", j=NJ)
        ff_t = area1[:, 2048:3072].rearrange("p (k t) -> p k t", k=PIECE)
        q_t = area2[:, 0:2048].rearrange("p (h t) -> p h t", h=AH)
        k_t = area2[:, 2048:4096].rearrange("p (h t) -> p h t", h=AH)
        half = NJ * MH * (MV + 1)
        mv = area2[:, 0:half].rearrange("p (j h d) -> p j h d", j=NJ, h=MH)
        hm = area2[:, half:2 * half].rearrange("p (j h d) -> p j h d", j=NJ, h=MH)
        ha_sq = area2[:, half:half + 2048].rearrange("p (j h d) -> p j h d", j=NJ, h=AH)
        o_sig = v_tok[:, :, :, :].rearrange("p j h d -> p (j h d)")[:, 0:2048].rearrange("p (j c) -> p j c", j=NJ)
        conv_x = area6[:, :].rearrange("p (c t) -> p c t", c=4)
        rope_a = area6[:, 0:512].rearrange("p (j h d) -> p j h d", j=NJ, h=4)
        rope_b = area6[:, 512:1024].rearrange("p (j h d) -> p j h d", j=NJ, h=4)
        g_row = area1[0:MH, 3072:3584].rearrange("p (k t) -> p k t", k=2)
        m_row = rope_w[0:MH, :, :, :].rearrange("p k j d -> p (k j d)").rearrange("p (k t) -> p k t", k=2)
        wg_raw = area1[:, 3328:3328 + KD * 8].rearrange("p (t c) -> p t c", t=KD)
        wg_hi = wg[:, 0:KD * 16].rearrange("p (t c) -> p t c", t=KD)[:, :, 0:8]
        wg_lo = wg[:, 0:KD * 16].rearrange("p (t c) -> p t c", t=KD)[:, :, 8:16]
        g_proj = area1[0:16, 3072:3072 + S]
        ident = con[:, K_ID:K_ID + P]
        upper = con[:, K_U:K_U + P]

        used = [0]

        def col(n):
            used[0] += n
            assert used[0] <= 256
            return small[:, used[0] - n:used[0]]

        ss1, r1, ss2, s2sum, r2 = col(2), col(2), col(8), col(2), col(2)
        qss, a_max, a_neg = col(8), col(2 * 2), col(2 * 2)
        a_ss, a_rd, a_r = col(16), col(16), col(16)
        z, lg, e_f, u_f, c_f, ru_f, ln_f, lf = col(16), col(16), col(8), col(8), col(8), col(8), col(8), col(8)
        m_exp, m_ss, m_den, m_rd, m_r = col(8), col(8), col(8), col(8), col(8)
        one = col(1)

        bank = [ctx.enter_context(nc.psum_tensor(f"bank{i}", [P, COLS], F32)) for i in range(8)]

        piece_landed = [sem(f"piece_landed{i}") for i in range(PIECES)]
        x_landed = [sem(f"x_landed{i}") for i in range(5)]
        chunk0_landed = sem("chunk0_landed")
        first_landed, con_landed, par_landed, side_landed = (sem("first_landed"), sem("con_landed"), sem("par_landed"),
                                                             sem("side_landed"))
        hi_ready, lo_ready, chunk_used = sem("hi_ready"), sem("lo_ready"), sem("chunk_used")
        padded = sem("padded")
        par_turned, par_ready = sem("par_turned"), sem("par_ready")
        x_turned, u_hi, u_lo = sem("x_turned"), sem("u_hi"), sem("u_lo")
        x_squared, x_mean, x_root, r1_ready = sem("x_squared"), sem("x_mean"), sem("x_root"), sem("r1_ready")
        r_spread, r_row_ready = sem("r_spread"), sem("r_row_ready")
        wg_hi_ready, wg_lo_ready = sem("wg_hi_ready"), sem("wg_lo_ready")
        evacuated = sem("evacuated")
        qk_squared, qk_mean, qk_root, roped = sem("qk_squared"), sem("qk_mean"), sem("qk_root"), sem("roped")
        qk_turned, qk_out = sem("qk_turned"), sem("qk_out")
        a_scored, a_masked, a_exped = sem("a_scored"), sem("a_masked"), sem("a_exped")
        a_turned, a_weighted, a_summed, a_out = sem("a_turned"), sem("a_weighted"), sem("a_summed"), sem("a_out")
        a_squared, a_mean, a_root, a_normed = sem("a_squared"), sem("a_mean"), sem("a_root"), sem("a_normed")
        ha_turned, ha_hi, ha_lo = sem("ha_turned"), sem("ha_hi"), sem("ha_lo")
        g_projected, g_copied = sem("g_projected"), sem("g_copied")
        g_summed, g_z, g_tanh, g_capped = sem("g_summed"), sem("g_z"), sem("g_tanh"), sem("g_capped")
        g_exped, g_plus1, g_logged, g_logf = sem("g_exped"), sem("g_plus1"), sem("g_logged"), sem("g_logf")
        g_turned, g_rows, m_scanned, m_turned, m_exped = (sem("g_turned"), sem("g_rows"), sem("m_scanned"),
                                                          sem("m_turned"), sem("m_exped"))
        seg_ready, d_summed, d_exped = sem("seg_ready"), sem("d_summed"), sem("d_exped")
        conv_x_ready, conv_first, conv_done, conv_silu = (sem("conv_x_ready"), sem("conv_first"), sem("conv_done"),
                                                          sem("conv_silu"))
        m_scored, m_decayed, m_summed, m_out = sem("m_scored"), sem("m_decayed"), sem("m_summed"), sem("m_out")
        m_squared, m_mean, m_root, m_normed = sem("m_squared"), sem("m_mean"), sem("m_root"), sem("m_normed")
        hm_turned, hm_hi, hm_lo = sem("hm_turned"), sem("hm_hi"), sem("hm_lo")
        out_added, h_squared, h_turned, u2_hi, u2_lo = (sem("out_added"), sem("h_squared"), sem("h_turned"),
                                                        sem("u2_hi"), sem("u2_lo"))
        h_mean, h_root, r2_ready = sem("h_mean"), sem("h_root"), sem("r2_ready")
        gated, ff_ready, ff_turned, ff_hi_ready, ff_lo_ready = (sem("gated"), sem("ff_ready"), sem("ff_turned"),
                                                                sem("ff_hi_ready"), sem("ff_lo_ready"))
        down_added, stored, settled = sem("down_added"), sem("stored"), sem("settled")
        last_summed, last_added = sem("last_summed"), sem("last_added")

        block = ctx.enter_context(nc.Block())

        @block.sync
        def _(sp):
            def load(p, src, slot):
                if not isinstance(p, int) or p >= PIECES:
                    sp.wait_ge(lo_ready, p * 2 - 2 * PIECES + 2)
                sp.dma_start(raw[:, slot, :, :], src).then_inc(piece_landed[slot], 16)

            def rows(w, first, c0):
                return w[0, first:first + PIECE * P, c0:c0 + COLS].rearrange("(t p) c -> p t c", p=P)

            def load_x(n):
                cols = slice(*X_PARTS[n:n + 2])
                sp.dma_start(h[:, :, cols], x[0, :, cols].rearrange("(j p) c -> p j c", p=P)).then_inc(x_landed[n], 16)

            def load_side():
                sp.dma_start(param_rows[0:8, :], attn_norm_w.rearrange("o h p -> (o h) p")).then_inc(par_landed, 16)
                sp.dma_start(param_rows[8:16, :], mlstm_norm_w.rearrange("o h (t p) -> (o h t) p", p=P)).then_inc(par_landed, 16)
                sp.dma_start(param_rows[16:32, :], norm2_w.rearrange("o (t p) -> (o t) p", p=P)).then_inc(par_landed, 16)
                sp.dma_start(param_rows[32:64, :], conv_w.rearrange("o w (t p) -> (o w t) p", p=P)).then_inc(par_landed, 16)
                sp.dma_start(param_rows[64:72, :], conv_b.rearrange("o (t p) -> (o t) p", p=P)).then_inc(par_landed, 16)
                sp.dma_start(con[:, P:K_ALL], consts[:, P:K_ALL]).then_inc(con_landed, 16)

            sp.dma_start(norm1_rows, norm1_w.rearrange("o (t p) -> (o t) p", p=P)).then_inc(first_landed, 16)
            sp.dma_start(con[:, 0:P], consts[:, 0:P]).then_inc(first_landed, 16)
            p = 0
            for c0 in IN_BLOCKS:
                for q in range(KD // PIECE):
                    if p == 0:
                        src = rows(w_in, 0, c0)
                        load_x(0)
                        sp.dma_start(raw[:, 0, 0:CHUNK, :], src[:, 0:CHUNK, :]).then_inc(chunk0_landed, 16)
                        load_x(1)
                        sp.dma_start(raw[:, 0, CHUNK:PIECE, :], src[:, CHUNK:PIECE, :]).then_inc(piece_landed[0], 16)
                    else:
                        if p < 4:
                            load_x(p + 1)
                        if p == 4:
                            load_side()
                        load(p, rows(w_in, q * PIECE * P, c0), p % PIECES)
                    p += 1
            for first in (D // 2, 0):
                for n in range(NB):
                    for q in range(KD // 2 // PIECE):
                        load(p, rows(w_out, first + q * PIECE * P, n * COLS), p % PIECES)
                        p += 1

            gate_v = w_gate[0].rearrange("(q t p) (g c) -> g q p t c", p=P, t=PIECE, c=COLS)
            up_v = w_up[0].rearrange("(q t p) (g c) -> g q p t c", p=P, t=PIECE, c=COLS)
            down_v = w_down[0].rearrange("(g t p) (n c) -> g n p t c", p=P, t=PIECE, c=COLS)

            for g in range(2):
                for v in (gate_v, up_v):
                    for q in range(4):
                        load(p, v[g, q], p % PIECES)
                        p += 1
            assert p == LOOP0 // 2
            with sp.Fori(1, GROUPS - 1) as i:
                for k, (v, g) in enumerate(((down_v, i - 1), (gate_v, i + 1), (up_v, i + 1))):
                    for q in range(4):
                        load(i * (PER_GROUP // 2) + (p - PER_GROUP // 2 + 4 * k + q), v[g, q], q)
            p = TAIL0 // 2
            for g in (GROUPS - 2, GROUPS - 1):
                for q in range(4):
                    load(p, down_v[g, q], p % PIECES)
                    p += 1
            for n in range(NB - 1):
                cols = slice(n * COLS, (n + 1) * COLS)
                sp.wait_ge(down_added, NB * (GROUPS - 1) + n + 1)
                sp.dma_start(out[0, :, cols].rearrange("(j p) c -> p j c", p=P), h[:, :, cols]).then_inc(stored, 16)
            for j in range(NJ):
                sp.wait_ge(last_added, j + 1)
                sp.dma_start(out[0, j * P:(j + 1) * P, D - COLS:D], h[:, j, D - COLS:D]).then_inc(stored, 16)
            sp.wait_ge(stored, 16 * (NB - 1 + NJ))

        @block.gpsimd
        def _(pool):
            pool.memset(one, 1.0).then_inc(padded, 1)
            pool.memset(v_tok[:, :, :, AD:AD + 1], 1.0).then_inc(padded, 1)
            pool.memset(wg[:, KD * 16:KD * 16 + P - 16].bitcast(F32), 0.0).then_inc(padded, 1)
            for n in range(5):
                pool.wait_ge(x_landed[n], 16)
            pool.dma_start(wg_raw, w_in[0, :, OFF_GATES:OFF_GATES + 8].rearrange("(t p) c -> p t c", p=P)
                           ).then_inc(side_landed, 16)
            pool.dma_start(gate_b[:, 0:MH], igate_b.partition_broadcast(P).rearrange("p o c -> p (o c)")
                           ).then_inc(side_landed, 16)
            pool.dma_start(gate_b[:, MH:8], fgate_b.partition_broadcast(P).rearrange("p o c -> p (o c)")
                           ).then_inc(side_landed, 16)
            pool.dma_start(qk_w[:, 0, :], q_norm_w.partition_broadcast(P).rearrange("p o c -> p (o c)")
                           ).then_inc(side_landed, 16)
            pool.dma_start(qk_w[:, 1, :], k_norm_w.partition_broadcast(P).rearrange("p o c -> p (o c)")
                           ).then_inc(side_landed, 16)

        @block.scalar
        def _(act):
            def split(c, landed, slot):
                if isinstance(c, int) and c < 2:
                    act.wait_ge((chunk0_landed, piece_landed[0])[c], 16)
                elif slot % 2 == 0:
                    act.wait_ge(piece_landed[slot // 2], landed)
                if not isinstance(c, int) or c >= CHUNKS_AHEAD:
                    act.wait_ge(chunk_used, c - (CHUNKS_AHEAD - 1))
                act.activation(w_hi[:, slot % 4, :, :], raw[:, slot // 2, 2 * (slot % 2):2 * (slot % 2) + 2, :],
                               ACT.Copy).then_inc(hi_ready, 1)

            def split_at(c):
                if c < CHUNKS:
                    split(c, 16 * (c // 8 + 1), c % 8)

            def u_part(c):
                act.wait_ge(x_turned, c + 1)
                for k in range(2):
                    act.activation(t_hi[:, 2 * c + k, :], bank[4 + c % 4][:, S * k:S * k + S], ACT.Copy,
                                   scale=par[:, C_N1 + 2 * c + k:C_N1 + 2 * c + k + 1]).then_inc(u_hi, 1)

            def ff_part(g, dst=ff_hi):
                act.wait_ge(ff_turned, (g + 1) * TURNS)
                act.activation(dst[:, 0:PIECE, :], ff_t, ACT.Copy).then_inc(ff_hi_ready, 1)

            def gate_silu(g):
                if not isinstance(g, int) or g:
                    act.wait_ge(ff_ready, g)
                for j in range(NJ):
                    act.activation(g_act[:, j, :], bank[j][:, :], ACT.Silu, scale=r2[:, j:j + 1]).then_inc(gated, 1)

            act.wait_ge(par_turned, 1)
            act.activation(par[:, 0:C_AN], bank[2][:, 0:C_AN], ACT.Copy).then_inc(par_ready, 1)
            act.wait_ge(par_ready, 1)
            for c in range(LEAD):
                u_part(c)
                split_at(c)
            for s in range(LOOP0):
                if s < 8 - LEAD:
                    u_part(s + LEAD)
                if s in (5, 6):
                    j = s - 5
                    for n in range(5):
                        act.wait_ge(x_landed[n], 16)
                    if j:
                        act.wait_ge(x_squared, j)
                    act.activation(squares, h[:, j, :], ACT.Square, accum_out=ss1[:, j:j + 1]).then_inc(x_squared, 1)
                if s == 7:
                    act.wait_ge(x_mean, 1)
                    act.activation(ss1, ss1, ACT.Sqrt).then_inc(x_root, 1)
                if s == 18:
                    act.wait_ge(side_landed, 16 * 5)
                    act.wait_ge(padded, 3)
                    act.activation(wg_hi, wg_raw, ACT.Copy).then_inc(wg_hi_ready, 1)
                if s == 12:
                    act.wait_ge(par_turned, 2)
                    act.activation(par[:, C_AN:C_ALL], bank[6][:, 0:C_ALL - C_AN], ACT.Copy).then_inc(par_ready, 1)
                if s in (18, 26, 34, 42):
                    b = s // 8 - 2
                    dst = q_t if b < 2 else k_t
                    for n in range(2):
                        act.wait_ge(qk_turned, 2 * b + n + 1)
                        act.activation(dst[:, 4 * (b % 2) + 2 * n:4 * (b % 2) + 2 * n + 2, :],
                                       bank[4 + n][:, :].rearrange("p (h t) -> p h t", h=2), ACT.Copy).then_inc(qk_out, 1)
                if s in (8, 16, 24, 32):
                    b = s // 8 - 1
                    act.wait_ge(chunk_used, s)
                    act.wait_ge(r1_ready, 1)
                    if b:
                        act.wait_ge(roped, b)
                    for j in range(NJ):
                        act.activation(tok[:, j, :, :], bank[2 * (b % 2) + j][:, :].rearrange("p (h d) -> p h d", h=4),
                                       ACT.Copy, scale=r1[:, j:j + 1]).then_inc(evacuated, 1)
                if s in (9, 17, 25, 33):
                    b = s // 8 - 1
                    act.wait_ge(evacuated, 2 * b + 2)
                    act.activation(sq, tok, ACT.Square).then_inc(qk_squared, 1)
                if s in (11, 19, 27, 35):
                    b = s // 8 - 1
                    act.wait_ge(qk_mean, b + 1)
                    act.activation(qss, qss, ACT.Sqrt).then_inc(qk_root, 1)
                if s in (40, 48):
                    b = s // 8 - 1
                    act.wait_ge(chunk_used, s)
                    act.wait_ge(padded, 3)
                    for j in range(NJ):
                        act.activation(v_tok[:, j, 4 * (b - 4):4 * (b - 4) + 4, 0:AD],
                                       bank[2 * (b % 2) + j][:, :].rearrange("p (h d) -> p h d", h=4),
                                       ACT.Copy, scale=r1[:, j:j + 1]).then_inc(evacuated, 1)
                if s >= NHEAD_SLOT + 7 and (s - NHEAD_SLOT) % 3 == 1 and (s - NHEAD_SLOT - 7) // 3 < AH:
                    n = (s - NHEAD_SLOT - 7) // 3
                    act.wait_ge(a_summed, n + 1)
                    act.activation(ha[:, :, n, :], bank[6][:, 0:2 * (AD + 1)].rearrange("p (j d) -> p j d", j=NJ),
                                   ACT.Copy).then_inc(a_out, 1)
                if s >= NHEAD_SLOT + 2 and (s - NHEAD_SLOT) % 3 == 2 and (s - NHEAD_SLOT - 2) // 3 < AH:
                    n = (s - NHEAD_SLOT - 2) // 3
                    act.wait_ge(a_masked, n + 1)
                    act.activation(sc[:, n % 2, 0:P], sc[:, n % 2, 0:P], ACT.Exp,
                                   bias=a_neg[:, 2 * (n % 2):2 * (n % 2) + 1]).then_inc(a_exped, 1)
                    act.activation(sc[:, n % 2, P:3 * P], sc[:, n % 2, P:3 * P], ACT.Exp,
                                   bias=a_neg[:, 2 * (n % 2) + 1:2 * (n % 2) + 2]).then_inc(a_exped, 1)
                if s == 73:
                    act.wait_ge(a_out, AH)
                    for j in range(NJ):
                        act.activation(ha_sq[:, j, :, :], ha[:, j, :, 0:AD], ACT.Square).then_inc(a_squared, 1)
                if s == 77:
                    act.wait_ge(a_mean, 1)
                    act.activation(a_ss, a_ss, ACT.Sqrt).then_inc(a_root, 1)
                if s in (81, 85):
                    n = (s - 81) // 4
                    for k in range(4):
                        if k % 2 == 0:
                            act.wait_ge(ha_turned, 2 * n + k // 2 + 1)
                        ch = 4 * n + k
                        act.activation(a_hi[:, ch, :], bank[5 + k // 2][:, S * (k % 2):S * (k % 2) + S], ACT.Copy,
                                       scale=par[:, C_AN + ch:C_AN + ch + 1]).then_inc(ha_hi, 1)
                if s == 47:
                    act.wait_ge(g_projected, 1)
                    act.activation(g_proj, bank[7][0:16, 0:S], ACT.Copy).then_inc(g_copied, 1)
                if s == 50:
                    act.wait_ge(g_z, 2)
                    act.activation(z, z, ACT.Tanh, scale=1.0 / GATE_CAP).then_inc(g_tanh, 1)
                if s == 52:
                    act.wait_ge(g_capped, 1)
                    act.activation(e_f.rearrange("p (j h) -> p j h", j=NJ),
                                   lg.rearrange("p (j h) -> p j h", j=NJ)[:, :, MH:8], ACT.Exp, scale=-1.0).then_inc(g_exped, 1)
                if s == 54:
                    act.wait_ge(g_plus1, 1)
                    act.activation(ln_f, u_f, ACT.Ln).then_inc(g_logged, 1)
                if s == 57:
                    act.wait_ge(g_turned, 1)
                    act.activation(g_row[:, 0:2, :], bank[7][0:MH, :].rearrange("p (k t) -> p k t", k=2), ACT.Copy).then_inc(g_rows, 1)
                if s == 61:
                    act.wait_ge(m_turned, 1)
                    act.activation(m_exp, bank[7][:, 0:8], ACT.Exp, scale=-1.0).then_inc(m_exped, 1)
                if s in (57, 65):
                    n = (s - 57) // 8
                    act.wait_ge(conv_x_ready, 2 * n + 2)
                    act.wait_ge(par_ready, 2)
                    for ct in range(4):
                        ch = 4 * n + ct
                        act.activation(mqk[:, ch, :], conv_x[:, ct, 0:S], ACT.Identity, bias=par[:, C_CB + ch:C_CB + ch + 1],
                                       scale=par[:, C_CW + ch:C_CW + ch + 1]).then_inc(conv_first, 1)
                if s in (62, 70):
                    n = (s - 62) // 8
                    act.wait_ge(conv_done, 4 * n + 4)
                    act.activation(mqk[:, 4 * n:4 * n + 4, :], mqk[:, 4 * n:4 * n + 4, :], ACT.Silu).then_inc(conv_silu, 1)
                if DEC_SLOT < s < DEC_SLOT + 2 * MH and (s - DEC_SLOT) % 2 == 1:
                    n = (s - DEC_SLOT) // 2
                    act.wait_ge(d_summed, n + 1)
                    act.activation(dec[:, n, 0:S], bank[7][:, 0:S], ACT.Exp, bias=lg[:, n:n + 1]).then_inc(d_exped, 1)
                    act.activation(dec[:, n, S:3 * P], bank[7][:, S:3 * P], ACT.Exp, bias=lg[:, 8 + n:8 + n + 1]).then_inc(d_exped, 1)
                if s in (72, 80):
                    n = (s - 72) // 8
                    act.wait_ge(chunk_used, s)
                    if n == 0:
                        act.wait_ge(padded, 4)
                    for j in range(NJ):
                        act.activation(mv[:, j, 2 * n:2 * n + 2, 0:MV], bank[2 * n + j][:, :].rearrange("p (h d) -> p h d", h=2),
                                       ACT.Copy, scale=r1[:, j:j + 1]).then_inc(evacuated, 1)
                if MP_SLOT < s < MP_SLOT + 2 * MH and (s - MP_SLOT) % 2 == 1:
                    n = (s - MP_SLOT) // 2
                    for j in range(NJ):
                        act.wait_ge(m_summed, 2 * n + j + 1)
                        act.activation(hm[:, j, n, :], bank[4 + 3 * j][:, 0:MV + 1], ACT.Copy).then_inc(m_out, 1)
                if s in (88, 96):
                    n = (s - 88) // 8
                    act.wait_ge(chunk_used, s)
                    if n == 0:
                        act.wait_ge(a_summed, AH)
                    for j in range(NJ):
                        act.activation(o_sig[:, j, COLS * n:COLS * n + COLS], bank[2 * n + j][:, :], ACT.Sigmoid,
                                       scale=r1[:, j:j + 1]).then_inc(evacuated, 1)
                if s == 90:
                    act.wait_ge(m_out, 2 * MH)
                    for j in range(NJ):
                        act.activation(squares[:, 1024 * j:1024 * j + 1024].rearrange("p (h d) -> p h d", h=MH),
                                       hm[:, j, :, 0:MV], ACT.Square).then_inc(m_squared, 1)
                if s == 93:
                    act.wait_ge(m_mean, 1)
                    act.activation(m_ss, m_ss, ACT.Sqrt).then_inc(m_root, 1)
                if 102 <= s < 102 + MH:
                    n = s - 102
                    act.wait_ge(hm_turned, n + 1)
                    for k in range(2):
                        act.activation(t_hi[:, 8 + 2 * n + k, :], bank[4 + n][:, S * k:S * k + S], ACT.Copy,
                                       scale=par[:, C_MN + 2 * n + k:C_MN + 2 * n + k + 1]).then_inc(hm_hi, 1)
                if s in (117, 121, 125, 129):
                    n = (s - 117) // 4
                    act.wait_ge(out_added, 4 + n + 1)
                    for j in range(NJ):
                        if 2 * n + j:
                            act.wait_ge(h_squared, 2 * n + j)
                        act.activation(squares[:, 0:COLS], h[:, j, COLS * n:COLS * n + COLS], ACT.Square,
                                       accum_out=ss2[:, 4 * j + n:4 * j + n + 1]).then_inc(h_squared, 1)
                if s in (119, 123, 127, 131):
                    n = (s - 119) // 4
                    for k in range(4):
                        if k % 2 == 0:
                            act.wait_ge(h_turned, 2 * n + k // 2 + 1)
                        kt = 4 * n + k
                        dst = t_hi[:, kt, :] if kt < 8 else a_hi[:, kt - 8, :]
                        act.activation(dst, bank[4 + 2 * (n % 2) + k // 2][:, S * (k % 2):S * (k % 2) + S], ACT.Copy,
                                       scale=par[:, C_N2 + kt:C_N2 + kt + 1]).then_inc(u2_hi, 1)
                if s == 132:
                    act.wait_ge(h_mean, 1)
                    act.activation(s2sum, s2sum, ACT.Sqrt).then_inc(h_root, 1)
                if s == G0 + 8:
                    act.wait_ge(chunk_used, U0)
                    act.wait_ge(r2_ready, 1)
                    gate_silu(0)
                if s == G1 + 8:
                    act.wait_ge(chunk_used, U1)
                    gate_silu(1)
                if s == G1 + 9:
                    ff_part(0)
                split_at(s + LEAD)

            def turn(i, first):
                for rel in range(PER_GROUP):
                    if rel == 17:
                        ff_part(i)
                    if rel == 16:
                        act.wait_ge(chunk_used, first + 16)
                        gate_silu(i + 1)
                    c = rel + LEAD
                    split(first + c, i * 48 + (16 * (LOOP0 // 8 + 1) - 48 + 16 * (c // 8)), c % 8)

            with act.Fori(1, GROUPS - 1) as i:
                turn(i, i * PER_GROUP + (LOOP0 - PER_GROUP))
            for s in range(TAIL0, CHUNKS):
                if s == TAIL0 + 6:
                    ff_part(GROUPS - 1, t_hi)
                split_at(s + LEAD)

        @block.tensor
        def _(pe):
            def product(ps, s_hi, s_lo, m_hi, m_lo, start, stop, skip=False):
                pe.matmul(ps, s_hi, m_hi, start=start, stop=False, skip_group_check=skip)
                pe.matmul(ps, s_hi, m_lo, start=False, stop=False, skip_group_check=skip)
                return pe.matmul(ps, s_lo, m_hi, start=False, stop=stop, skip_group_check=skip)

            def tile_of(kt, kind):
                if kind == "u":
                    return t_hi[:, kt, :], t_lo[:, kt, :]
                if kind == "u2":
                    return (t_hi[:, kt, :], t_lo[:, kt, :]) if kt < 8 else (a_hi[:, kt - 8, :], a_lo[:, kt - 8, :])
                if kind == "attention":
                    return a_hi[:, kt, :], a_lo[:, kt, :]
                if kind == "mlstm":
                    return t_hi[:, 8 + kt, :], t_lo[:, 8 + kt, :]
                if kind == "last hidden":
                    return t_hi[:, kt, :], t_lo[:, kt, :]
                return ff_hi[:, kt, :], ff_lo[:, kt, :]

            def chunk(c, slot, q, last, pair, kind):
                pe.wait_ge(lo_ready, c + 1)
                for k in range(CHUNK):
                    a_h, a_l = tile_of(CHUNK * q + k, kind)
                    for j in range(NJ):
                        mm = product(bank[pair + j][:, :], a_h[:, j * P:j * P + P], a_l[:, j * P:j * P + P],
                                     w_hi[:, slot, k, :], w_lo[:, slot, k, :],
                                     start=(q == 0 and k == 0), stop=(q == last and k == CHUNK - 1))
                mm.then_inc(chunk_used, 1)

            def chunk_by_channel(c, slot, q, pair):
                pe.wait_ge(lo_ready, c + 1)
                for k in range(CHUNK):
                    kt = CHUNK * q + k
                    for ct in range(4):
                        mm = product(bank[pair + ct // 2][:, S * (ct % 2):S * (ct % 2) + S],
                                     w_hi[:, slot, k, P * ct:P * ct + P], w_lo[:, slot, k, P * ct:P * ct + P],
                                     t_hi[:, kt, :], t_lo[:, kt, :],
                                     start=(kt == 0 and ct % 2 == 0), stop=(kt == KD - 1), skip=True)
                mm.then_inc(chunk_used, 1)

            def turn_x(c):
                if 256 * c in X_PARTS:
                    pe.wait_ge(x_landed[X_PARTS.index(256 * c)], 16)
                if c >= 4:
                    pe.wait_ge(u_lo, 2 * (c - 4) + 2)
                for k in range(2):
                    for j in range(NJ):
                        kt = 2 * c + k
                        mm = pe.transpose(bank[4 + c % 4][:, S * k + P * j:S * k + P * j + P],
                                          h[:, j, P * kt:P * kt + P], ident)
                mm.then_inc(x_turned, 1)

            pe.wait_ge(first_landed, 32)
            pe.transpose(bank[2][:, 0:C_AN], norm1_rows, con[0:C_AN, K_ID:K_ID + C_AN]).then_inc(par_turned, 1)
            turn_x(0)
            turn_x(1)

            for s in range(LOOP0):
                if 1 <= s <= 6:
                    turn_x(s + 1)
                if s == 10:
                    pe.wait_ge(par_landed, 16 * 5)
                    n = C_ALL - C_AN
                    pe.transpose(bank[6][:, 0:n], param_rows, con[0:n, K_ID:K_ID + n]).then_inc(par_turned, 1)
                if s == 13:
                    pe.wait_ge(r1_ready, 1)
                    for j in range(NJ):
                        mm = pe.matmul(bank[7][:, P * j:P * j + P], r1[:, j:j + 1].broadcast_to([P, P]), ident,
                                       start=True, stop=True)
                    mm.then_inc(r_spread, 1)
                if s in (17, 25, 33, 41):
                    b = s // 8 - 2
                    pe.wait_ge(roped, b + 1)
                    if b:
                        pe.wait_ge(qk_out, 2 * b)
                    for n in range(2):
                        for k in range(2):
                            for j in range(NJ):
                                mm = pe.transpose(bank[4 + n][:, S * k + P * j:S * k + P * j + P],
                                                  rot[:, j, 2 * n + k, :], ident)
                        mm.then_inc(qk_turned, 1)
                if s >= NHEAD_SLOT + 6 and (s - NHEAD_SLOT) % 3 == 0 and (s - NHEAD_SLOT - 6) // 3 < AH:
                    n = (s - NHEAD_SLOT - 6) // 3
                    pe.wait_ge(a_weighted, n + 1)
                    pe.wait_ge(evacuated, 10 if n < 4 else 12)
                    if n:
                        pe.wait_ge(a_out, n)
                    pe.matmul(bank[6][:, 0:AD + 1], p_t[:, 0:P], v_tok[:, 0, n, :], start=True, stop=True)
                    pe.matmul(bank[6][:, AD + 1:2 * AD + 2], p_t[:, P:2 * P], v_tok[:, 0, n, :], start=True, stop=False)
                    pe.matmul(bank[6][:, AD + 1:2 * AD + 2], p_t[:, 2 * P:3 * P], v_tok[:, 1, n, :],
                              start=False, stop=True).then_inc(a_summed, 1)
                if s >= NHEAD_SLOT + 4 and (s - NHEAD_SLOT) % 3 == 1 and (s - NHEAD_SLOT - 4) // 3 < AH:
                    n = (s - NHEAD_SLOT - 4) // 3
                    pe.wait_ge(a_exped, 2 * n + 2)
                    if n:
                        pe.wait_ge(a_weighted, n)
                    else:
                        pe.wait_ge(qk_out, 8)
                    for k in range(3):
                        mm = pe.transpose(bank[5][:, P * k:P * k + P], sc[:, n % 2, P * k:P * k + P], ident)
                    mm.then_inc(a_turned, 1)
                if s >= NHEAD_SLOT and (s - NHEAD_SLOT) % 3 == 0 and (s - NHEAD_SLOT) // 3 < AH:
                    n = (s - NHEAD_SLOT) // 3
                    if n == 0:
                        pe.wait_ge(qk_out, 8)
                    else:
                        pe.wait_ge(a_masked, n)
                    pe.matmul(bank[4][:, 0:P], q_t[:, n, 0:P], k_t[:, n, 0:P], start=True, stop=True)
                    pe.matmul(bank[4][:, P:3 * P], q_t[:, n, P:S], k_t[:, n, :], start=True, stop=True).then_inc(a_scored, 1)
                if s in (80, 84):
                    n = (s - 80) // 4
                    pe.wait_ge(a_normed, 2)
                    if n:
                        pe.wait_ge(ha_lo, 4)
                    for b in range(2):
                        for k in range(2):
                            for j in range(NJ):
                                mm = pe.transpose(bank[5 + b][:, S * k + P * j:S * k + P * j + P],
                                                  ha[:, j, 4 * n + 2 * b + k, 0:AD], ident)
                        mm.then_inc(ha_turned, 1)
                if s == 46:
                    pe.wait_ge(con_landed, 16)
                    pe.wait_ge(wg_lo_ready, 1)
                    pe.wait_ge(r_row_ready, 1)
                    for kt in range(KD):
                        w = wg[:, 16 * kt:16 * kt + P]
                        pe.matmul(bank[7][:, 0:S], w, t_hi[:, kt, :], start=(kt == 0), stop=False)
                        mm = pe.matmul(bank[7][:, 0:S], w, t_lo[:, kt, :], start=False, stop=(kt == KD - 1))
                    mm.then_inc(g_projected, 1)
                if s == 48:
                    pe.wait_ge(g_copied, 1)
                    for j in range(NJ):
                        mm = pe.transpose(bank[7][:, 16 * j:16 * j + 16], g_proj[:, P * j:P * j + P], con[0:16, K_ID:K_ID + 16])
                    mm.then_inc(g_summed, 1)
                if s == 56:
                    pe.wait_ge(g_logf, 1)
                    for j in range(NJ):
                        pe.transpose(bank[7][0:MH, P * j:P * j + P], lf[:, MH * j:MH * j + MH], ident)
                        mm = pe.transpose(bank[7][0:MH, S + P * j:S + P * j + P], lg[:, 8 * j:8 * j + MH], ident)
                    mm.then_inc(g_turned, 1)
                if s == 60:
                    pe.wait_ge(m_scanned, 2)
                    for j in range(NJ):
                        mm = pe.transpose(bank[7][:, MH * j:MH * j + MH], m_row[:, 0, P * j:P * j + P], con[0:MH, K_ID:K_ID + MH])
                    mm.then_inc(m_turned, 1)
                if DEC_SLOT <= s < DEC_SLOT + 2 * MH and (s - DEC_SLOT) % 2 == 0:
                    n = (s - DEC_SLOT) // 2
                    pe.wait_ge(seg_ready, 2 * n + 2)
                    if n == 0:
                        pe.wait_ge(m_exped, 1)
                    else:
                        pe.wait_ge(d_exped, 2 * n)
                    pick = con[0:MH, K_ID + n:K_ID + n + 1].broadcast_to([MH, P])
                    for j, ps in ((0, bank[7][:, 0:P]), (1, bank[7][:, 2 * P:3 * P])):
                        pe.matmul(ps, seg[:, j, n, :], upper, start=True, stop=False)
                        pe.matmul(ps, ident, con[:, K_NU:K_NU + P], start=False, stop=False)
                        mm = pe.matmul(ps, pick, m_row[:, 1, P * j:P * j + P], start=False, stop=True)
                    ps = bank[7][:, P:2 * P]
                    pe.matmul(ps, seg[:, 0, n, :], one.broadcast_to([P, P]), start=True, stop=False)
                    pe.matmul(ps, lf[:, MH + n:MH + n + 1].broadcast_to([P, P]), upper, start=False, stop=False)
                    pe.matmul(ps, pick, m_row[:, 1, P:S], start=False, stop=True).then_inc(d_summed, 1)
                if MS_SLOT <= s < MS_SLOT + 2 * MH and (s - MS_SLOT) % 2 == 0:
                    n = (s - MS_SLOT) // 2
                    if n == 0:
                        pe.wait_ge(d_exped, 2 * MH)
                        pe.wait_ge(conv_silu, 2)
                    else:
                        pe.wait_ge(m_decayed, n)
                    pe.matmul(bank[7][:, 0:S], mqk[:, 4 + n, 0:P], mqk[:, n, :], start=True, stop=True)
                    pe.matmul(bank[7][:, S:3 * P], mqk[:, 4 + n, P:S], mqk[:, n, P:S], start=True, stop=True).then_inc(m_scored, 1)
                if MP_SLOT <= s < MP_SLOT + 2 * MH and (s - MP_SLOT) % 2 == 0:
                    n = (s - MP_SLOT) // 2
                    pe.wait_ge(m_decayed, MH)
                    pe.wait_ge(evacuated, 16 if n >= 2 else 14)
                    if n:
                        pe.wait_ge(m_out, 2 * n)
                    pe.matmul(bank[4][:, 0:MV + 1], dec[:, n, 0:P], mv[:, 0, n, :], start=True, stop=True).then_inc(m_summed, 1)
                    pe.matmul(bank[7][:, 0:MV + 1], dec[:, n, P:S], mv[:, 0, n, :], start=True, stop=False)
                    pe.matmul(bank[7][:, 0:MV + 1], dec[:, n, S:3 * P], mv[:, 1, n, :], start=False, stop=True).then_inc(m_summed, 1)
                if s == 101:
                    pe.wait_ge(m_normed, 2 * MH)
                    pe.wait_ge(ha_lo, 8)
                    for n in range(MH):
                        for k in range(2):
                            for j in range(NJ):
                                mm = pe.transpose(bank[4 + n][:, S * k + P * j:S * k + P * j + P],
                                                  hm[:, j, n, P * k:P * k + P], ident)
                        mm.then_inc(hm_turned, 1)
                if s in (118, 122, 126, 130):
                    n = (s - 118) // 4
                    pe.wait_ge(out_added, 4 + n + 1)
                    if n < 2:
                        pe.wait_ge(hm_lo, 8)
                    else:
                        pe.wait_ge(u2_lo, 4 * (n - 1))
                    for b in range(2):
                        for k in range(2):
                            for j in range(NJ):
                                kt = 4 * n + 2 * b + k
                                mm = pe.transpose(bank[4 + 2 * (n % 2) + b][:, S * k + P * j:S * k + P * j + P],
                                                  h[:, j, P * kt:P * kt + P], ident)
                        mm.then_inc(h_turned, 1)

                if s < OUT0:
                    b, q = s // IN_CH, s % IN_CH
                    if b == 0:
                        pe.wait_ge(u_lo, 2 * q + 2)
                    if q == 0 and b >= 2:
                        if b < 8:
                            pe.wait_ge(evacuated, 2 * (b - 1))
                        elif b in (8, 9):
                            pe.wait_ge(conv_x_ready, 2 * (b - 7))
                        else:
                            pe.wait_ge(evacuated, 12 + 2 * (b - 9))
                    if q == 0 and b == 1:
                        pe.wait_ge(par_ready, 1)
                    if b in (6, 7):
                        chunk_by_channel(s, s % 4, q, 2 * (b % 2))
                    else:
                        chunk(s, s % 4, q, IN_CH - 1, 2 * (b % 2), "u")
                elif s < FFN0:
                    m, q = (s - OUT0) // OUT_CH, (s - OUT0) % OUT_CH
                    if q == 0:
                        if m < 2:
                            pe.wait_ge(evacuated, 18 + 2 * m)
                        else:
                            pe.wait_ge(out_added, m - 1)
                        pe.wait_ge(ha_lo, 8)
                        if m == NB:
                            pe.wait_ge(hm_lo, 8)
                    chunk(s, s % 4, q, OUT_CH - 1, 2 * (m % 2), "attention" if m < NB else "mlstm")
                else:
                    m, q = (s - FFN0) // IN_CH, (s - FFN0) % IN_CH
                    if m == 0:
                        if q == 0:
                            pe.wait_ge(out_added, 7)
                        pe.wait_ge(u2_lo, 4 * (q // 2) + 4)
                    if m == 1 and q == 0:
                        pe.wait_ge(out_added, 8)
                    if m == 2 and q == 0:
                        pe.wait_ge(gated, 2)
                    if m == 3 and q == 0:
                        pe.wait_ge(ff_ready, 1)
                    chunk(s, s % 4, q, IN_CH - 1, 2 * (m % 2), "u2")

            def down(g, first, kind="hidden"):
                pe.wait_ge(ff_lo_ready, g + 1)
                for n in range(NB):
                    if not isinstance(g, int) or g:
                        pe.wait_ge(down_added, g * NB + n - 1)
                    elif n >= 2:
                        pe.wait_ge(down_added, n - 1)
                    if kind == "last hidden" and n == NB - 1:
                        last_block()
                        continue
                    for q in range(2):
                        chunk(first + (2 * n + q), (2 * n + q) % 4, q, 1, 4 + 2 * (n % 2), kind)

            def last_block():
                pe.wait_ge(lo_ready, CHUNKS)
                for j in range(NJ):
                    for q in range(2):
                        for k in range(CHUNK):
                            a_h, a_l = tile_of(CHUNK * q + k, "last hidden")
                            slot = (CHUNKS - 2 + q) % 4
                            mm = product(bank[6 + j][:, :], a_h[:, j * P:j * P + P], a_l[:, j * P:j * P + P],
                                         w_hi[:, slot, k, :], w_lo[:, slot, k, :],
                                         start=(q == 0 and k == 0), stop=(q == 1 and k == CHUNK - 1))
                    mm.then_inc(last_summed, 1)

            def turn(i, first):
                down(i - 1, first)
                pe.wait_ge(gated, i * 2 + 2)
                for q in range(IN_CH):
                    chunk(first + (IN_CH + q), q % 4, q, IN_CH - 1, 0, "u2")
                pe.wait_ge(ff_ready, i + 1)
                for q in range(IN_CH):
                    chunk(first + (2 * IN_CH + q), q % 4, q, IN_CH - 1, 2, "u2")

            turn(1, LOOP0)
            with pe.Fori(2, GROUPS - 1) as i:
                turn(i, i * PER_GROUP + (LOOP0 - PER_GROUP))
            down(GROUPS - 2, TAIL0)
            down(GROUPS - 1, TAIL0 + IN_CH, kind="last hidden")

        @block.vector
        def _(dve):
            steps = [0]

            def settle(ins):
                steps[0] += 1
                ins.then_inc(settled, 1)
                dve.wait_ge(settled, steps[0])

            def split(c, slot):
                dve.wait_ge(hi_ready, c + 1)
                dve.tensor_tensor(w_lo[:, slot % 4, :, :], raw[:, slot // 2, 2 * (slot % 2):2 * (slot % 2) + 2, :],
                                  w_hi[:, slot % 4, :, :].bitcast(F32), ALU.subtract).then_inc(lo_ready, 1)

            def split_at(c):
                if c < CHUNKS:
                    split(c, c % 8)

            def low_part(dst, ps, scale, hi):
                return dve.scalar_tensor_tensor(out=dst, in0=ps, scalar=scale, in1=hi.bitcast(F32),
                                                op0=ALU.mult, op1=ALU.subtract)

            def u_part(c):
                for k in range(2):
                    kt = 2 * c + k
                    dve.wait_ge(u_hi, 2 * c + 2)
                    low_part(t_lo[:, kt, :], bank[4 + c % 4][:, S * k:S * k + S], par[:, C_N1 + kt:C_N1 + kt + 1],
                             t_hi[:, kt, :]).then_inc(u_lo, 1)

            def turn_ff(g, first, last):
                if first == 0:
                    dve.wait_ge(ff_ready, g + 1)
                    if not isinstance(g, int) or g:
                        dve.wait_ge(ff_lo_ready, g)
                for n in range(first, last):
                    a, b = 32 * (n // 4), 32 * (n % 4)
                    dve.transpose(ff_t[b:b + 32, :, :].rearrange("p k (j t) -> p j k t", j=NJ)[:, :, :, a:a + 32],
                                  ff[a:a + 32, :, :].rearrange("p j (k c) -> p j k c", k=PIECE)[:, :, :, b:b + 32]
                                  ).then_inc(ff_turned, 1)

            def ff_part(g, dst=ff_lo, hi=ff_hi):
                dve.wait_ge(ff_hi_ready, g + 1)
                dve.tensor_tensor(dst[:, 0:PIECE, :], ff_t, hi[:, 0:PIECE, :].bitcast(F32), ALU.subtract).then_inc(ff_lo_ready, 1)

            def hidden(g):
                dve.wait_ge(gated, g * 2 + 2)
                for j in range(NJ):
                    mm = dve.scalar_tensor_tensor(out=ff[:, j, :], in0=bank[2 + j][:, :], scalar=r2[:, j:j + 1],
                                                  in1=g_act[:, j, :], op0=ALU.mult, op1=ALU.mult)
                mm.then_inc(ff_ready, 1)

            def add_block(n, pair, signal):
                for j in range(NJ):
                    hb = h[:, j, COLS * n:COLS * n + COLS]
                    mm = dve.tensor_tensor(hb, bank[pair + j][:, :], hb, ALU.add)
                mm.then_inc(signal, 1)

            def rope_table(n):
                for k, (w0, base) in enumerate(((0, K_COS), (64, K_SIN), (64, K_COS), (0, K_SIN))):
                    mm = dve.tensor_tensor(rope_w[:, k, :, :], con[:, base:base + 128].rearrange("p (j d) -> p j d", j=NJ),
                                           qk_w[:, n:n + 1, w0:w0 + 64].broadcast_to([P, NJ, 64]), ALU.mult)
                settle(mm)

            def mean_of(dst, src, n):
                return dve.tensor_scalar(dst, src, 1.0 / n, EPS, ALU.mult, ALU.add)

            dve.wait_ge(par_ready, 1)
            for c in range(LEAD):
                u_part(c)
                split_at(c)
            for s in range(LOOP0):
                if s < 8 - LEAD:
                    u_part(s + LEAD)
                if s == 7:
                    dve.wait_ge(x_squared, 2)
                    mean_of(ss1, ss1, D).then_inc(x_mean, 1)
                if s == 8:
                    dve.wait_ge(x_root, 1)
                    dve.reciprocal(r1, ss1).then_inc(r1_ready, 1)
                if s == 8:
                    dve.wait_ge(con_landed, 16)
                    dve.wait_ge(side_landed, 16 * 5)
                    rope_table(0)
                if s == 19:
                    dve.wait_ge(wg_hi_ready, 1)
                    dve.tensor_tensor(wg_lo, wg_raw, wg_hi.bitcast(F32),
                                      ALU.subtract).then_inc(wg_lo_ready, 1)
                if s == 15:
                    dve.wait_ge(r_spread, 1)
                    dve.tensor_copy(r_row[:, :], bank[7][:, 0:S]).then_inc(r_row_ready, 1)
                if s == 24:
                    dve.wait_ge(roped, 2)
                    rope_table(1)
                if s in (10, 18, 26, 34):
                    b = s // 8 - 1
                    dve.wait_ge(qk_squared, b + 1)
                    settle(dve.tensor_reduce(qss, sq.rearrange("p j h d -> p (j h) d"), AX.X, ALU.add))
                    mean_of(qss, qss, AD).then_inc(qk_mean, 1)
                if s in (12, 20, 28, 36):
                    b = s // 8 - 1
                    dve.wait_ge(qk_root, b + 1)
                    settle(dve.reciprocal(qss, qss))
                    t3 = tok.rearrange("p j h d -> p (j h) d")
                    settle(dve.tensor_tensor(t3, t3, qss.unsqueeze(2).broadcast_to([P, 8, AD]), ALU.mult))
                if s in (13, 21, 29, 37):
                    b = s // 8 - 1
                    if b:
                        dve.wait_ge(qk_turned, 2 * b)
                    def wide(k):
                        return rope_w[:, k, :, :].unsqueeze(2).broadcast_to([P, NJ, 4, 64])
                    dve.tensor_tensor(rope_a, tok[:, :, :, 0:64], wide(0), ALU.mult)
                    settle(dve.tensor_tensor(rope_b, tok[:, :, :, 64:128], wide(1), ALU.mult))
                    settle(dve.tensor_tensor(rot[:, :, :, 0:64], rope_a, rope_b, ALU.subtract))
                if s in (14, 22, 30, 38):
                    dve.tensor_tensor(rope_a, tok[:, :, :, 64:128], wide(2), ALU.mult)
                    settle(dve.tensor_tensor(rope_b, tok[:, :, :, 0:64], wide(3), ALU.mult))
                    dve.tensor_tensor(rot[:, :, :, 64:128], rope_a, rope_b, ALU.add).then_inc(roped, 1)
                if s == 41:
                    dve.wait_ge(roped, 4)
                    settle(dve.memset(conv_x[:, :, 0:3], 0.0))
                if s >= NHEAD_SLOT + 5 and (s - NHEAD_SLOT) % 3 == 2 and (s - NHEAD_SLOT - 5) // 3 < AH:
                    n = (s - NHEAD_SLOT - 5) // 3
                    dve.wait_ge(a_turned, n + 1)
                    if n:
                        dve.wait_ge(a_summed, n)
                    dve.tensor_tensor(p_t[:, :], bank[5][:, 0:3 * P], con[:, K_W:K_W + 3 * P], ALU.mult).then_inc(a_weighted, 1)
                if s >= NHEAD_SLOT + 1 and (s - NHEAD_SLOT) % 3 == 1 and (s - NHEAD_SLOT - 1) // 3 < AH:
                    n = (s - NHEAD_SLOT - 1) // 3
                    m = n % 2
                    dve.wait_ge(a_scored, n + 1)
                    if n >= 2:
                        dve.wait_ge(a_turned, n - 1)
                    dve.tensor_tensor_reduce(sc[:, m, 0:P], bank[4][:, 0:P], con[:, K_NEG + P:K_NEG + 2 * P], AD ** -0.5,
                                             -3.0e38, ALU.add, ALU.max, a_max[:, 2 * m:2 * m + 1])
                    settle(dve.tensor_tensor_reduce(sc[:, m, P:3 * P], bank[4][:, P:3 * P], con[:, K_NEG:K_NEG + 2 * P],
                                                    AD ** -0.5, -3.0e38, ALU.add, ALU.max, a_max[:, 2 * m + 1:2 * m + 2]))
                    dve.tensor_scalar(a_neg[:, 2 * m:2 * m + 2], a_max[:, 2 * m:2 * m + 2], -1.0, None,
                                      ALU.mult).then_inc(a_masked, 1)
                if s == 75:
                    dve.wait_ge(a_squared, 2)
                    dve.tensor_reduce(a_ss, ha_sq.rearrange("p j h d -> p (j h) d"), AX.X, ALU.add)
                    settle(dve.reciprocal(a_rd, ha[:, :, :, AD]))
                    settle(dve.tensor_tensor(a_ss, a_ss, a_rd, ALU.mult))
                    settle(dve.tensor_tensor(a_ss, a_ss, a_rd, ALU.mult))
                    mean_of(a_ss, a_ss, AD).then_inc(a_mean, 1)
                if s == 78:
                    dve.wait_ge(a_root, 1)
                    settle(dve.reciprocal(a_r, a_ss))
                    settle(dve.tensor_tensor(a_r, a_r, a_rd, ALU.mult))
                if s in (78, 79):
                    for j in (s - 78,):
                        dve.tensor_tensor(ha[:, j, :, 0:AD], ha[:, j, :, 0:AD],
                                          a_r[:, AH * j:AH * j + AH].unsqueeze(2).broadcast_to([P, AH, AD]),
                                          ALU.mult).then_inc(a_normed, 1)
                if s in (82, 86):
                    n = (s - 82) // 4
                    for k in range(4):
                        ch = 4 * n + k
                        dve.wait_ge(ha_hi, 4 * n + 2 * (k // 2) + 2)
                        low_part(a_lo[:, ch, :], bank[5 + k // 2][:, S * (k % 2):S * (k % 2) + S],
                                 par[:, C_AN + ch:C_AN + ch + 1], a_hi[:, ch, :]).then_inc(ha_lo, 1)
                if s == 49:
                    dve.wait_ge(g_summed, 1)
                    parts = bank[7][:, 0:32].rearrange("p (j k c) -> p j k c", j=NJ, k=2)
                    settle(dve.tensor_reduce(z, parts.rearrange("p j k c -> p j c k"), AX.X, ALU.add))
                    for j in range(NJ):
                        zj = z[:, 8 * j:8 * j + 8]
                        dve.scalar_tensor_tensor(out=zj, in0=zj, scalar=r1[:, j:j + 1], in1=gate_b[:, :], op0=ALU.mult,
                                                 op1=ALU.add).then_inc(g_z, 1)
                if s == 51:
                    dve.wait_ge(g_tanh, 1)
                    dve.tensor_scalar(lg, z, GATE_CAP, None, ALU.mult).then_inc(g_capped, 1)
                if s == 53:
                    dve.wait_ge(g_exped, 1)
                    settle(dve.tensor_scalar(u_f, e_f, 1.0, None, ALU.add))
                    dve.tensor_scalar(c_f, u_f, -1.0, None, ALU.add).then_inc(g_plus1, 1)
                    settle(dve.reciprocal(ru_f, u_f))
                    settle(dve.tensor_tensor(c_f, e_f, c_f, ALU.subtract))
                    settle(dve.tensor_tensor(c_f, c_f, ru_f, ALU.mult))
                if s == 55:
                    dve.wait_ge(g_logged, 1)
                    settle(dve.tensor_tensor(lf, ln_f, c_f, ALU.add))
                    dve.tensor_scalar(lf, lf, -1.0, None, ALU.mult).then_inc(g_logf, 1)
                if s == 58:
                    dve.wait_ge(g_rows, 1)
                    dve.tensor_tensor_scan(m_row[:, 0, :], g_row[:, 0, :], g_row[:, 1, :], 0.0, ALU.add, ALU.max
                                           ).then_inc(m_scanned, 1)
                    dve.wait_ge(m_scanned, 1)
                    dve.tensor_scalar(m_row[:, 1, :], m_row[:, 0, :], -1.0, None, ALU.mult).then_inc(m_scanned, 1)
                if s in (59, 60, 62, 63):
                    n = (59, 60, 62, 63).index(s)
                    dve.wait_ge(g_logf, 1)
                    for j in range(NJ):
                        dve.tensor_scalar(seg[:, j, n, :], con[:, K_L:K_L + P], lf[:, MH * j + n:MH * j + n + 1], None,
                                          ALU.mult).then_inc(seg_ready, 1)
                if s in (56, 64):
                    n = (s - 56) // 8
                    dve.wait_ge(chunk_used, s)
                    for b in range(2):
                        dve.tensor_tensor(conv_x[:, 2 * b:2 * b + 2, 3:3 + S],
                                          bank[2 * n + b][:, :].rearrange("p (c t) -> p c t", c=2),
                                          r_row[:, :].unsqueeze(1).broadcast_to([P, 2, S]), ALU.mult).then_inc(conv_x_ready, 1)
                if 58 <= s <= 61 or 66 <= s <= 69:
                    n, ct = (s - 58) // 8, (s - 58) % 8
                    ch = 4 * n + ct
                    dve.wait_ge(conv_first, ch + 1)
                    for t in range(1, 4):
                        mm = dve.scalar_tensor_tensor(out=mqk[:, ch, :], in0=conv_x[:, ct, t:t + S],
                                                      scalar=par[:, C_CW + 8 * t + ch:C_CW + 8 * t + ch + 1],
                                                      in1=mqk[:, ch, :], op0=ALU.mult, op1=ALU.add)
                        if t < 3:
                            settle(mm)
                    mm.then_inc(conv_done, 1)
                if MS_SLOT < s < MS_SLOT + 2 * MH and (s - MS_SLOT) % 2 == 1:
                    n = (s - MS_SLOT) // 2
                    dve.wait_ge(m_scored, n + 1)
                    dve.scalar_tensor_tensor(out=dec[:, n, :], in0=bank[7][:, 0:3 * P], scalar=MQ ** -0.5, in1=dec[:, n, :],
                                             op0=ALU.mult, op1=ALU.mult).then_inc(m_decayed, 1)
                if s == 67:
                    dve.wait_ge(a_scored, AH)
                    dve.memset(mv[:, :, :, MV:MV + 1], 1.0).then_inc(padded, 1)
                if s == 91:
                    dve.wait_ge(m_squared, 2)
                    dve.wait_ge(m_exped, 1)
                    m3 = m_den.rearrange("p (j h) -> p j h", j=NJ)
                    dve.tensor_reduce(m_ss, squares.rearrange("p (k d) -> p k d", d=MV), AX.X, ALU.add)
                    settle(dve.tensor_scalar(m3, hm[:, :, :, MV], -1.0, None, ALU.mult))
                    settle(dve.tensor_tensor(m3, m3, hm[:, :, :, MV], ALU.max))
                    settle(dve.tensor_tensor(m_den, m_den, m_exp, ALU.max))
                    settle(dve.reciprocal(m_rd, m_den))
                    settle(dve.tensor_tensor(m_ss, m_ss, m_rd, ALU.mult))
                    settle(dve.tensor_tensor(m_ss, m_ss, m_rd, ALU.mult))
                    mean_of(m_ss, m_ss, MV).then_inc(m_mean, 1)
                if s == 94:
                    dve.wait_ge(m_root, 1)
                    settle(dve.reciprocal(m_r, m_ss))
                    settle(dve.tensor_tensor(m_r, m_r, m_rd, ALU.mult))
                if s in (97, 98):
                    j = s - 97
                    dve.wait_ge(evacuated, 20)
                    for n in range(MH):
                        dve.scalar_tensor_tensor(out=hm[:, j, n, 0:MV], in0=hm[:, j, n, 0:MV],
                                                 scalar=m_r[:, MH * j + n:MH * j + n + 1],
                                                 in1=o_sig[:, j, MV * n:MV * n + MV], op0=ALU.mult, op1=ALU.mult
                                                 ).then_inc(m_normed, 1)
                if 103 <= s < 103 + MH:
                    n = s - 103
                    dve.wait_ge(hm_hi, 2 * n + 2)
                    for k in range(2):
                        kt = 2 * n + k
                        low_part(t_lo[:, 8 + kt, :], bank[4 + n][:, S * k:S * k + S], par[:, C_MN + kt:C_MN + kt + 1],
                                 t_hi[:, 8 + kt, :]).then_inc(hm_lo, 1)
                if OUT0 + 4 <= s <= FFN0 and s % 4 == 0:
                    m = (s - OUT0) // 4 - 1
                    dve.wait_ge(chunk_used, s)
                    if m == 0:
                        dve.wait_ge(x_squared, 2)
                    if m >= NB:
                        dve.wait_ge(out_added, m - NB + 1)
                    add_block(m % NB, 2 * (m % 2), out_added)
                if s in (120, 124, 128, 132):
                    n = (s - 120) // 4
                    for k in range(4):
                        kt = 4 * n + k
                        dve.wait_ge(u2_hi, 4 * n + 2 * (k // 2) + 2)
                        d_hi, d_lo = (t_hi[:, kt, :], t_lo[:, kt, :]) if kt < 8 else (a_hi[:, kt - 8, :], a_lo[:, kt - 8, :])
                        low_part(d_lo, bank[4 + 2 * (n % 2) + k // 2][:, S * (k % 2):S * (k % 2) + S],
                                 par[:, C_N2 + kt:C_N2 + kt + 1], d_hi).then_inc(u2_lo, 1)
                if s == 131:
                    dve.wait_ge(h_squared, 8)
                    settle(dve.tensor_reduce(s2sum, ss2.rearrange("p (j n) -> p j n", j=NJ), AX.X, ALU.add))
                    mean_of(s2sum, s2sum, D).then_inc(h_mean, 1)
                if s == 133:
                    dve.wait_ge(h_root, 1)
                    dve.reciprocal(r2, s2sum).then_inc(r2_ready, 1)
                if s == U0 + 8:
                    dve.wait_ge(chunk_used, G1)
                    dve.wait_ge(r2_ready, 1)
                    hidden(0)
                if G1 < s <= G1 + 8:
                    turn_ff(0, 2 * (s - G1) - 2, 2 * (s - G1))
                if s == G1 + 10:
                    ff_part(0)
                split_at(s + LEAD)

            def turn(i, first, tail=False):
                dve.wait_ge(chunk_used, first)
                dve.wait_ge(ff_turned, i * TURNS)
                hidden(i)
                for rel in range(PER_GROUP):
                    if rel in (2, 4, 6, 8):
                        n = rel // 2 - 1
                        dve.wait_ge(chunk_used, first + rel)
                        dve.wait_ge(out_added, 2 * NB)
                        if not isinstance(i, int) or i > 1:
                            dve.wait_ge(down_added, i * NB + (n + 1 - 2 * NB))
                        add_block(n, 4 + 2 * (n % 2), down_added)
                    if 9 <= rel <= 16:
                        turn_ff(i, 2 * (rel - 9), 2 * (rel - 8))
                    if rel == 18:
                        ff_part(i)
                    c = rel + LEAD
                    split(first + c, c % 8)

            turn(1, LOOP0)
            with dve.Fori(2, GROUPS - 1) as i:
                turn(i, i * PER_GROUP + (LOOP0 - PER_GROUP))
            for s in range(TAIL0, CHUNKS + 1):
                rel = s - TAIL0
                if rel == 0:
                    dve.wait_ge(chunk_used, s)
                    dve.wait_ge(ff_turned, TURNS * (GROUPS - 1))
                    hidden(GROUPS - 1)
                if 1 <= rel <= 5:
                    turn_ff(GROUPS - 1, (0, 4, 6, 10, 12)[rel - 1], (4, 6, 10, 12, 16)[rel - 1])
                if rel == 7:
                    ff_part(GROUPS - 1, t_lo, t_hi)
                if rel >= 2 and rel % 2 == 0:
                    m = NB * (GROUPS - 2) + rel // 2 - 1
                    dve.wait_ge(down_added, m + 1 - NB)
                    if s < CHUNKS:
                        dve.wait_ge(chunk_used, s)
                        add_block(m % NB, 4 + 2 * (m % 2), down_added)
                    else:
                        for j in range(NJ):
                            dve.wait_ge(last_summed, j + 1)
                            hb = h[:, j, D - COLS:D]
                            dve.tensor_tensor(hb, bank[6 + j][:, :], hb, ALU.add).then_inc(last_added, 1)
                split_at(s + LEAD)


_NAMES = ["x", "norm1_w", "w_in", "conv_w", "conv_b", "igate_b", "fgate_b", "q_norm_w", "k_norm_w",
          "mlstm_norm_w", "attn_norm_w", "w_out", "norm2_w", "w_gate", "w_up", "w_down"]


def kernel(**inputs):
    import concourse.bacc as bacc
    from concourse.bass_utils import run_bass_kernel_spmd

    nc = bacc.Bacc("TRN2", target_bir_lowering=False, num_devices=1)
    arrays = {name: np.ascontiguousarray(inputs[name]) for name in _NAMES}
    arrays["shape_consts"] = constants()
    args = [nc.dram_tensor(name, a.shape, mybir.dt.from_np(a.dtype), kind="ExternalInput").ap()
            for name, a in arrays.items()]
    out = nc.dram_tensor("out", (1, S, D), F32, kind="ExternalOutput").ap()
    build(nc, *args, out)
    return run_bass_kernel_spmd(nc, [arrays], core_ids=[0]).results[0]["out"]
```
